# Optimizing a Trainium2 kernel written in Bass

```python
import math
import jax, jax.numpy as jnp
from jax import lax
import numpy as np

D_MODEL = 2048
BATCH = 1
SEQ = 256
DEPTH = 1

CHUNK = 64
EPS = 1e-6
NEG_INF = -1e30

D_MIX = D_MODEL
DIFF_WIDTH = D_MIX // 2
GMLP_WIDTH = D_MIX - DIFF_WIDTH

DIFF_HEADS = 8
DIFF_QK_DIM = DIFF_WIDTH // DIFF_HEADS // 2
DIFF_V_DIM = 2 * DIFF_QK_DIM
ROPE_DIMS = DIFF_QK_DIM // 4
ROPE_THETA = 500000.0
Q_BLOCK = 128

GMLP_GROUPS = 8
GMLP_GROUP_CH = GMLP_WIDTH // GMLP_GROUPS
GMLP_LEN = 128

Q_COLS = DIFF_HEADS * 2 * DIFF_QK_DIM
K_COLS = DIFF_HEADS * 2 * DIFF_QK_DIM
V_COLS = DIFF_HEADS * DIFF_V_DIM
U_COLS = GMLP_WIDTH
Z_COLS = GMLP_WIDTH
IN_COLS = Q_COLS + K_COLS + V_COLS + U_COLS + Z_COLS

PEER_HEADS = 8
PEER_N_KEYS = 128
PEER_N_EXPERTS = PEER_N_KEYS * PEER_N_KEYS
PEER_QUERY_DIM = 256
PEER_HALF = PEER_QUERY_DIM // 2
PEER_TOPK = 16
PEER_TOKEN_BLOCK = 128

kernel_name = "hymba_diffattn_gmlp_peer_block"

def rmsnorm(x, g):
    xf = x.astype(jnp.float32)
    y = xf * lax.rsqrt(jnp.mean(xf * xf, axis=-1, keepdims=True) + EPS)
    return (y * g.astype(jnp.float32)).astype(x.dtype)

def rope_tables(seq_len, dtype):
    pos = jnp.arange(seq_len, dtype=jnp.float32)
    inv_freq = ROPE_THETA ** (-jnp.arange(0, ROPE_DIMS, 2, dtype=jnp.float32) / ROPE_DIMS)
    ang = pos[:, None] * inv_freq[None, :]
    return jnp.cos(ang).astype(dtype), jnp.sin(ang).astype(dtype)

def apply_partial_rope(t, cos, sin):
    half = ROPE_DIMS // 2
    c = cos[None, :, None, None, :]
    s = sin[None, :, None, None, :]
    x1 = t[..., :half]
    x2 = t[..., half:ROPE_DIMS]
    return jnp.concatenate([x1 * c - x2 * s, x2 * c + x1 * s, t[..., ROPE_DIMS:]], axis=-1)

def diff_attention(q, k, v, lam, subln_g, lambda_init):
    B, S = q.shape[0], q.shape[1]
    nqb = S // Q_BLOCK
    qb = q.reshape(B, nqb, Q_BLOCK, DIFF_HEADS, 2, DIFF_QK_DIM).transpose(1, 0, 3, 4, 2, 5)
    kt = k.transpose(0, 2, 3, 1, 4)
    vt = v.transpose(0, 2, 1, 3)
    chunk_id = jnp.arange(S, dtype=jnp.int32) // CHUNK
    q_chunk = chunk_id.reshape(nqb, Q_BLOCK)
    scale = DIFF_QK_DIM ** -0.5

    def one_block(args):
        q_blk, q_ch = args
        s = jnp.einsum('bhmqd,bhmkd->bhmqk', q_blk, kt).astype(jnp.float32) * scale
        mask = chunk_id[None, :] <= q_ch[:, None]
        s = jnp.where(mask, s, NEG_INF)
        p = jax.nn.softmax(s, axis=-1)
        a = p[:, :, 0] - lam * p[:, :, 1]
        return jnp.einsum('bhqk,bhkd->bhqd', a.astype(vt.dtype), vt)

    o = lax.map(one_block, (qb, q_chunk))
    o = o.transpose(1, 0, 3, 2, 4).reshape(B, S, DIFF_HEADS, DIFF_V_DIM)
    o = rmsnorm(o, subln_g) * (1.0 - lambda_init)
    return o.reshape(B, S, DIFF_WIDTH)

def gmlp_spatial_gating(u, z, z_norm_g, w_s, b_s):
    B, S = u.shape[0], u.shape[1]
    u = jax.nn.gelu(u)
    z = jax.nn.gelu(z).reshape(B, S, GMLP_GROUPS, GMLP_GROUP_CH)
    z = rmsnorm(z, z_norm_g.reshape(GMLP_GROUPS, GMLP_GROUP_CH))
    z = z.reshape(B, S // GMLP_LEN, GMLP_LEN, GMLP_GROUPS, GMLP_GROUP_CH)
    pos_chunk = jnp.arange(GMLP_LEN, dtype=jnp.int32) // CHUNK
    mask = pos_chunk[:, None] >= pos_chunk[None, :]
    w = jnp.where(mask[None], w_s, jnp.zeros_like(w_s))
    sz = jnp.einsum('gpq,bnqgc->bnpgc', w, z) + b_s.T[None, None, :, :, None]
    return u * sz.reshape(B, S, GMLP_WIDTH)

def peer_ffn(x, w_q, sub_keys, u_tab, v_tab):
    B, S, D = x.shape
    xt = x.reshape(-1, PEER_TOKEN_BLOCK, D)

    def one_block(xb):
        T = xb.shape[0]
        q = (xb @ w_q).reshape(T, PEER_HEADS, 2, PEER_HALF)
        sc = jnp.einsum('thcd,hckd->thck', q, sub_keys)
        s1, i1 = lax.top_k(sc[:, :, 0], PEER_TOPK)
        s2, i2 = lax.top_k(sc[:, :, 1], PEER_TOPK)
        cand = (s1[..., :, None] + s2[..., None, :]).reshape(T, PEER_HEADS, PEER_TOPK * PEER_TOPK)
        best, ci = lax.top_k(cand, PEER_TOPK)
        e1 = jnp.take_along_axis(i1, ci // PEER_TOPK, axis=-1)
        e2 = jnp.take_along_axis(i2, ci % PEER_TOPK, axis=-1)
        idx = e1 * PEER_N_KEYS + e2
        g = jax.nn.softmax(best.astype(jnp.float32), axis=-1)
        u_sel = jnp.take(u_tab, idx, axis=0)
        act = jax.nn.gelu(jnp.einsum('td,thkd->thk', xb, u_sel))
        v_sel = jnp.take(v_tab, idx, axis=0)
        return jnp.einsum('thk,thkd->td', g.astype(act.dtype) * act, v_sel)

    out = lax.map(one_block, xt)
    return out.reshape(B, S, D)

def setup_inputs(seed: int = 0) -> dict:
    key = jax.random.key(seed)
    ks = jax.random.split(key, 20)
    f32 = jnp.float32
    nrm = lambda k, shape, s: jax.random.normal(k, shape, f32) * s
    gain = lambda k, shape: 1.0 + 0.02 * jax.random.normal(k, shape, f32)
    return {
        "x": jax.random.normal(ks[0], (BATCH, SEQ, D_MODEL), f32),
        "mix_norm_g": gain(ks[1], (DEPTH, D_MODEL)),
        "w_in": nrm(ks[2], (DEPTH, D_MODEL, IN_COLS), D_MODEL ** -0.5),
        "lambda_q1": nrm(ks[3], (DEPTH, DIFF_QK_DIM), 0.1),
        "lambda_k1": nrm(ks[4], (DEPTH, DIFF_QK_DIM), 0.1),
        "lambda_q2": nrm(ks[5], (DEPTH, DIFF_QK_DIM), 0.1),
        "lambda_k2": nrm(ks[6], (DEPTH, DIFF_QK_DIM), 0.1),
        "subln_g": gain(ks[7], (DEPTH, DIFF_V_DIM)),
        "gmlp_z_norm_g": gain(ks[8], (DEPTH, GMLP_WIDTH)),
        "gmlp_w_s": nrm(ks[9], (DEPTH, GMLP_GROUPS, GMLP_LEN, GMLP_LEN), GMLP_LEN ** -0.5),
        "gmlp_b_s": gain(ks[10], (DEPTH, GMLP_GROUPS, GMLP_LEN)),
        "gmlp_out_g": gain(ks[11], (DEPTH, GMLP_WIDTH)),
        "w_out": nrm(ks[12], (DEPTH, D_MIX, D_MODEL), D_MIX ** -0.5),
        "ffn_norm_g": gain(ks[13], (DEPTH, D_MODEL)),
        "peer_w_q": nrm(ks[14], (DEPTH, D_MODEL, PEER_HEADS * PEER_QUERY_DIM), D_MODEL ** -0.5),
        "peer_sub_keys": nrm(ks[15], (DEPTH, PEER_HEADS, 2, PEER_N_KEYS, PEER_HALF), PEER_HALF ** -0.5),
        "peer_u": nrm(ks[16], (DEPTH, PEER_N_EXPERTS, D_MODEL), D_MODEL ** -0.5),
        "peer_v": nrm(ks[17], (DEPTH, PEER_N_EXPERTS, D_MODEL), 0.3),
        "final_norm_g": gain(ks[18], (D_MODEL,)),
    }

def reference(x, mix_norm_g, w_in, lambda_q1, lambda_k1, lambda_q2, lambda_k2, subln_g,
              gmlp_z_norm_g, gmlp_w_s, gmlp_b_s, gmlp_out_g, w_out, ffn_norm_g,
              peer_w_q, peer_sub_keys, peer_u, peer_v, final_norm_g):
    B, S = x.shape[0], x.shape[1]
    cos, sin = rope_tables(S, x.dtype)
    splits = [Q_COLS, Q_COLS + K_COLS, Q_COLS + K_COLS + V_COLS, Q_COLS + K_COLS + V_COLS + U_COLS]
    for l in range(DEPTH):
        lambda_init = 0.8 - 0.6 * math.exp(-0.3 * l)
        hn = rmsnorm(x, mix_norm_g[l])
        proj = hn @ w_in[l]
        q, k, v, u_g, z_g = jnp.split(proj, splits, axis=-1)
        q = apply_partial_rope(q.reshape(B, S, DIFF_HEADS, 2, DIFF_QK_DIM), cos, sin)
        k = apply_partial_rope(k.reshape(B, S, DIFF_HEADS, 2, DIFF_QK_DIM), cos, sin)
        v = v.reshape(B, S, DIFF_HEADS, DIFF_V_DIM)
        lam = (jnp.exp(jnp.sum(lambda_q1[l].astype(jnp.float32) * lambda_k1[l].astype(jnp.float32)))
               - jnp.exp(jnp.sum(lambda_q2[l].astype(jnp.float32) * lambda_k2[l].astype(jnp.float32)))
               + lambda_init)
        attn_out = diff_attention(q, k, v, lam, subln_g[l], lambda_init)
        gmlp_out = rmsnorm(gmlp_spatial_gating(u_g, z_g, gmlp_z_norm_g[l], gmlp_w_s[l], gmlp_b_s[l]),
                           gmlp_out_g[l])
        mixed = jnp.concatenate([attn_out, gmlp_out], axis=-1) @ w_out[l]
        x = x + mixed
        x = x + peer_ffn(rmsnorm(x, ffn_norm_g[l]), peer_w_q[l], peer_sub_keys[l], peer_u[l], peer_v[l])
    return rmsnorm(x, final_norm_g)


_drawn_inputs = setup_inputs


def setup_inputs(seed=0):
    import zlib

    import numpy as np

    out = dict(_drawn_inputs(seed))
    spreads = {}
    factors = {'lambda_q1': 3.294,
     'lambda_q2': 64.0,
     'subln_g': 12.623,
     'gmlp_z_norm_g': 21.557,
     'gmlp_b_s': 18.962,
     'gmlp_out_g': 10.647,
     'ffn_norm_g': 11.407,
     'final_norm_g': 8.046}
    for name, (base, spread) in spreads.items():
        noise = np.random.default_rng([zlib.crc32(name.encode()), seed]).standard_normal(out[name].shape)
        drawn = base * np.exp(spread * noise) if base else spread * noise
        out[name] = __import__('jax').numpy.asarray(drawn.astype(out[name].dtype))
    for name, factor in factors.items():
        out[name] = (out[name] * factor).astype(out[name].dtype)
    return out
```

```python
import math

import numpy as np
import concourse.bass as bass
from concourse import mybir
from contextlib import ExitStack

FP32 = mybir.dt.float32
FP32R = mybir.dt.float32r
U32 = mybir.dt.uint32
ALU = mybir.AluOpType
ACT = mybir.ActivationFunctionType
AX = mybir.AxisListType

P = 128
T, D = 256, 2048
TT = T // P
KT = D // P
HALF = D // 2
BANK = 512
HEADS, QK, VD = 8, 64, 128
ROT = 8
CHUNK = 64
GROUPS = 8
EPS = 1e-6
LAMBDA_INIT = 0.8 - 0.6 * math.exp(-0.3 * 0)
PH, TOPK, NKEYS = 8, 16, 128
HC = 2 * PH
FLOOR = -3.0e38
NEG = -1e30

UNIT = 1024
N_PROJ, N_OUT, N_WQ, N_U, N_V = 5 * KT, 2 * KT, 2 * HC, 2 * NKEYS, 2 * NKEYS
OUT0 = N_PROJ
WQ0 = OUT0 + N_OUT
U0 = WQ0 + N_WQ
V0 = U0 + N_U
END = V0 + N_V
RAW_SLOTS, HI_SLOTS, LO_SLOTS = 4, 4, 2
VG = 8
N_VG = NKEYS // VG
Z_, U_, Q_, K_, V_ = range(5)
COLS = {Z_: 4096, U_: 3072, Q_: 0, K_: 1024, V_: 2048}
TOK8 = 8


def hybrid_peer_block(nc, x, w_in, w_out, wq_t, keys_t, u_t, peer_v, ws_t, bs_t, gain_t, z_gain, out_gain,
                      subln_gain, final_gain, lambdas, rope, out):
    ctx = ExitStack()
    with ctx:
        base = (nc.sbuf_base + 63) // 64 * 64

        def at(name, off, shape, dt=FP32):
            return nc.alloc_sbuf_tensor_at(name, shape, dt, offset=base + off)

        def sem(name):
            return ctx.enter_context(nc.semaphore(name))

        KB = 1024
        store = at("store", 0, [P, NKEYS, T])
        X = at("X", 0, [P, TT, D])
        GRP = at("GRP", 16 * KB, [P, 5, TT, HALF])
        MIX = at("MIX", 56 * KB, [P, TT, D])
        QT = at("QT", 72 * KB, [P, HEADS, T])
        KTr = at("KTr", 80 * KB, [P, HEADS, T])
        S = at("S", 88 * KB, [P, 2, 2, T])
        PR = at("PR", 92 * KB, [P, 2, 2, T])
        AM = at("AM", 96 * KB, [P, 2, T])
        AT = at("AT", 98 * KB, [P, 2, 2, P])
        MASK = at("MASK", 100 * KB, [P, TT, T])
        XS = at("XS", 72 * KB, [P, TT, D])
        SQ = at("SQ", 102 * KB, [P, TT, HALF])
        ZG = at("ZG", 110 * KB, [P, HALF])
        OG = at("OG", 114 * KB, [P, HALF])
        WST = at("WST", 118 * KB, [P, GROUPS, P])
        SG = at("SG", 122 * KB, [P, VD])
        LAMV = at("LAMV", 123 * KB, [P, 4, QK])
        ROPE = at("ROPE", 124 * KB, [P, 2, TT, ROT])
        RT = at("RT", 88 * KB, [P, 4, 2 * HC, ROT])
        JUNK = at("JUNK", 102 * KB, [P, D])
        SC = at("SC", 64 * KB, [P, TT, HC, NKEYS])
        QTQ = at("QTQ", 80 * KB, [P, HC, T])
        KEYS = at("KEYS", 96 * KB, [P, HC, NKEYS])
        CAND = at("CAND", 104 * KB, [P, PH, TOPK, TOPK])
        EQ = at("EQ", 112 * KB, [P, PH, TOPK, TOPK])
        S16 = at("S16", 120 * KB, [P, TT, HC, TOPK])
        I16 = at("I16", 122 * KB, [P, TT, HC, TOPK], U32)
        I16F = at("I16F", 124 * KB, [P, TT, HC, TOPK])
        BEST = at("BEST", 126 * KB, [P, PH, TOPK])
        CI = at("CI", 126 * KB + 512, [P, PH, TOPK], U32)
        CIA = at("CIA", 127 * KB, [P, PH, TOPK], U32)
        CF = at("CF", 127 * KB + 512, [P, PH, TOPK])
        xT = at("xT", 128 * KB, [P, KT, 2, T], FP32R)
        ACC = at("ACC", 128 * KB, [P, TT, D])
        WHL = at("WHL", 144 * KB, [P, VG, 2, T], FP32R)
        ONE1 = at("ONE1", 144 * KB, [P, 2, TOK8, NKEYS])
        ONE2 = at("ONE2", 152 * KB, [P, 2, TOK8, NKEYS])
        FG = at("FG", 0, [P, D])
        FJ = at("FJ", 8 * KB, [P, D])
        RAW = at("RAW", 160 * KB, [P, RAW_SLOTS, UNIT])
        HI = at("HI", 176 * KB, [P, HI_SLOTS, UNIT], FP32R)
        LO = at("LO", 192 * KB, [P, LO_SLOTS, UNIT], FP32R)
        off = [200 * KB]

        def small(name, shape, dt=FP32):
            n = 4 * int(np.prod(shape[1:]))
            t = at(name, off[0], shape, dt)
            off[0] += (n + 31) // 32 * 32
            return t

        IDENT = small("IDENT", [P, P])
        IOTA = small("IOTA", [P, NKEYS])
        EG = small("EG", [P, 3, T])
        ROWS = small("ROWS", [P, 3, PH * TOPK])
        GT = small("GT", [P, 2, KT])
        BS = small("BS", [P, GROUPS])
        SS = small("SS", [P, 8])
        GS = small("GS", [P, 3, TT, GROUPS])
        LAM = small("LAM", [P, 8])
        NB = small("NB", [P, 2, 2])
        LS = small("LS", [P, 2, 2])
        RL = small("RL", [P, 2, 2])
        GM = small("GM", [P, 3, PH])

        PS = ctx.enter_context(nc.psum_tensor("PS", [P, 8, BANK], FP32))
        x1_dram = nc.dram_tensor("x1_spill", [T, D], FP32).ap()

        raw_ready = [sem(f"raw_ready{i}") for i in range(RAW_SLOTS)]
        hi_ready, lo_ready, used = sem("hi_ready"), sem("lo_ready"), sem("used")
        x_ready, small_ready = sem("x_ready"), sem("small_ready")
        consts = sem("consts")
        act_chain, dve_chain = sem("act_chain"), sem("dve_chain")
        sums = sem("sums")
        means = sem("means")
        roots = sem("roots")
        rows_ready = sem("rows_ready")
        tr_done, tr_hi, tr_lo = sem("tr_done"), sem("tr_hi"), sem("tr_lo")
        evac = sem("evac")
        z_ready, sz_done, sz_read = sem("z_ready"), sem("sz_done"), sem("sz_read")
        roped, qk_tr, qk_out = sem("roped"), sem("qk_tr"), sem("qk_out")
        scored, shifted, maxed, exped = sem("scored"), sem("shifted"), sem("maxed"), sem("exped")
        lam_sums, lam_exp, mixed_probs = sem("lam_sums"), sem("lam_exp"), sem("mixed_probs")
        at_done, at_out, pv_done, pv_out = sem("at_done"), sem("at_out"), sem("pv_done"), sem("pv_out")
        x1_ready, x1_saved, x1_back = sem("x1_ready"), sem("x1_saved"), sem("x1_back")
        tile_out = sem("tile_out")
        keys_ready = sem("keys_ready")
        sc_done, sc_out = sem("sc_done"), sem("sc_out")
        best_ready, gexp = sem("best_ready"), sem("gexp")
        picks, picks_tr, picks_out = sem("picks"), sem("picks_tr"), sem("picks_out")
        gelus = sem("gelus")
        one1, one2, one2g, g_done, g_read = sem("one1"), sem("one2"), sem("one2g"), sem("g_done"), sem("g_read")
        w_hi, w_lo, flushed = sem("w_hi"), sem("w_lo"), sem("flushed")
        fg_ready, fin, stored = sem("fg_ready"), sem("fin"), sem("stored")

        v_view = peer_v.rearrange("(e j) d -> e j d", j=NKEYS)
        N_SMALL = 10

        block = ctx.enter_context(nc.Block())

        @block.sync
        def _(sp):
            def load(n, slot, src):
                if not isinstance(n, int) or n >= RAW_SLOTS:
                    sp.wait_ge(lo_ready, n - (RAW_SLOTS - 1))
                sp.dma_start(RAW[:, slot, :], src).then_inc(raw_ready[slot], 16)

            for g in range(5):
                for k in range(KT):
                    n = g * KT + k
                    load(n, n % RAW_SLOTS, w_in[k * P:(k + 1) * P, COLS[g]:COLS[g] + UNIT])
            for g in range(2):
                for k in range(KT):
                    n = OUT0 + g * KT + k
                    load(n, n % RAW_SLOTS, w_out[k * P:(k + 1) * P, g * UNIT:(g + 1) * UNIT])
            for u in range(N_WQ):
                load(WQ0 + u, u % RAW_SLOTS, wq_t[u // 2, :, (u % 2) * UNIT:(u % 2 + 1) * UNIT])
            with sp.Fori(0, N_U // 4) as i:
                for r in range(4):
                    load(i * 4 + (U0 + r), r,
                         u_t[bass.ds(i * 2 + r // 2, 1), :, (r % 2) * UNIT:(r % 2 + 1) * UNIT]
                         .rearrange("a p n -> p (a n)"))
            with sp.Fori(0, N_VG) as g:
                for u in range(2 * VG):
                    h, jj = divmod(u, VG)
                    load(g * (2 * VG) + (V0 + u), u % RAW_SLOTS,
                         v_view[:, bass.ds(g * VG + jj, 1), h * UNIT:(h + 1) * UNIT]
                         .rearrange("p a n -> p (a n)"))
            sp.wait_ge(fin, TT)
            for tt in range(TT):
                sp.dma_start(out[tt * P:(tt + 1) * P, :], ACC[:, tt, :]).then_inc(stored, 16)
            sp.wait_ge(stored, 16 * TT)

        @block.gpsimd
        def _(pool):
            for tt in range(TT):
                pool.dma_start(X[:, tt, :], x[tt * P:(tt + 1) * P, :]).then_inc(x_ready, 16)
            nc.gpsimd.memset(IDENT[:], 0.0).then_inc(consts, 1)
            nc.gpsimd.iota(IOTA[:], [[1, NKEYS]], base=0, channel_multiplier=0,
                           allow_small_or_imprecise_dtypes=True).then_inc(consts, 1)
            nc.gpsimd.memset(MASK[:], 0.0).then_inc(consts, 1)
            pool.wait_ge(consts, 3)
            nc.gpsimd.affine_select(out=IDENT[:], in_=IDENT[:], compare_op=ALU.not_equal, fill=1.0, base=0,
                                    pattern=[[-1, P]], channel_multiplier=1).then_inc(consts, 1)
            pool.wait_ge(consts, 4)
            for n, tt in enumerate(range(TT)):
                nc.gpsimd.memset(MASK[0:CHUNK, tt, P * tt + CHUNK:T], NEG).then_inc(consts, 1)
                pool.wait_ge(consts, 5 + n)
            nc.gpsimd.memset(MASK[CHUNK:P, 0, P:T], NEG).then_inc(consts, 1)
            pool.wait_ge(consts, 7)
            loads = [
                (GT[:], gain_t), (BS[:], bs_t), (WST[:], ws_t),
                (ZG[:], z_gain.broadcast_to([P, HALF])), (OG[:], out_gain.broadcast_to([P, HALF])),
                (SG[:], subln_gain.broadcast_to([P, VD])),
                (LAMV[:].rearrange("p a b -> p (a b)"), lambdas.broadcast_to([P, 4 * QK])),
                (ROPE[:], rope),
            ]
            for dst, src in loads:
                pool.dma_start(dst, src).then_inc(small_ready, 16)
            pool.wait_ge(small_ready, 16 * len(loads))
            nc.gpsimd.memset(WST[CHUNK:P, :, 0:CHUNK], 0.0).then_inc(consts, 1)
            pool.wait_ge(tr_lo, 24)
            pool.dma_start(KEYS[:], keys_t).then_inc(keys_ready, 16)
            pool.wait_ge(x1_ready, 8)
            for tt in range(TT):
                pool.dma_start(x1_dram[tt * P:(tt + 1) * P, :], X[:, tt, :]).then_inc(x1_saved, 16)
            pool.wait_ge(x1_saved, 16 * TT)
            pool.wait_ge(used, V0)
            for tt in range(TT):
                pool.dma_start(ACC[:, tt, :], x1_dram[tt * P:(tt + 1) * P, :]).then_inc(x1_back, 16)
            pool.wait_ge(picks_out, TT)
            with pool.Fori(0, T // (2 * TOK8)) as i:
                for s in range(2):
                    pool.wait_ge(one2, i * 2 + (s + 1))
                    nc.gpsimd.tensor_tensor(
                        ONE2[:, s], ONE2[:, s],
                        EG[:, 2, bass.ds(i * 16 + 8 * s, TOK8)].unsqueeze(2).broadcast_to([P, TOK8, NKEYS]),
                        ALU.mult).then_inc(one2g, 1)
            pool.wait_ge(used, V0 + 16 * 8)
            pool.dma_start(FG[:], final_gain.broadcast_to([P, D])).then_inc(fg_ready, 16)

        @block.scalar
        def _(act):
            chain = [0]

            def link(ins):
                chain[0] += 1
                ins.then_inc(act_chain, 1)
                act.wait_ge(act_chain, chain[0])

            def hi(n, s4):
                if isinstance(n, int):
                    act.wait_ge(raw_ready[s4], 16 * (n // RAW_SLOTS + 1))
                    if n >= HI_SLOTS:
                        act.wait_ge(used, n - (HI_SLOTS - 1))
                nc.scalar.activation(HI[:, s4, :], RAW[:, s4, :], ACT.Copy).then_inc(hi_ready, 1)

            def hi_at(it, per, first, u):
                act.wait_ge(raw_ready[u % 4], it * (4 * per) + 16 * ((first + u) // 4 + 1))
                act.wait_ge(used, it * per + (first + u - (HI_SLOTS - 1)))
                nc.scalar.activation(HI[:, u % 4, :], RAW[:, u % 4, :], ACT.Copy).then_inc(hi_ready, 1)

            n_sums = [0]

            def squares(src, col, junk):
                if n_sums[0]:
                    act.wait_ge(sums, n_sums[0])
                n_sums[0] += 1
                nc.scalar.activation(junk, src, ACT.Square, accum_out=SS[:, col:col + 1]).then_inc(sums, 1)

            def root(count, dst, src):
                act.wait_ge(means, count)
                nc.scalar.activation(dst, src, ACT.Sqrt).then_inc(roots, 1)

            def transposed_hi(rnd, gain):
                for kp in range(KT // 2):
                    act.wait_ge(tr_done, 8 * rnd + kp + 1)
                    for k in (2 * kp, 2 * kp + 1):
                        src = PS[:, kp, (k % 2) * T:(k % 2 + 1) * T]
                        if gain is None:
                            ins = nc.scalar.activation(xT[:, k, 0, :], src, ACT.Copy)
                        else:
                            ins = nc.scalar.activation(xT[:, k, 0, :], src, ACT.Copy, scale=GT[:, gain, k:k + 1])
                    ins.then_inc(tr_hi, 1)

            for n in range(4):
                hi(n, n)
            act.wait_ge(x_ready, 16 * TT)
            for tt in range(TT):
                squares(X[:, tt, :], tt, JUNK[:])
            root(1, SS[:, 2:4], SS[:, 2:4])
            act.wait_ge(small_ready, 16 * 8)
            transposed_hi(0, 0)

            def copy_out(g):
                for tt in range(TT):
                    for c in range(2):
                        act.wait_ge(used, KT * (g + 1))
                        nc.scalar.activation(GRP[:, g, tt, c * BANK:(c + 1) * BANK], PS[:, 4 * (g % 2) + 2 * tt + c, :],
                                             ACT.Gelu_apprx_tanh if g in (Z_, U_) else ACT.Copy).then_inc(evac, 1)

            for n in range(4, N_PROJ + 4):
                hi(n, n % 4)
                if n % KT == 3 and n > KT:
                    copy_out(n // KT - 1)
                if n == 2 * KT + 8:
                    root(2, GS[:, 1], GS[:, 1])
            act.wait_ge(lam_sums, 1)
            nc.scalar.activation(LAM[:, 2:4], LAM[:, 0:2], ACT.Exp).then_inc(lam_exp, 1)
            for b in range(8):
                act.wait_ge(qk_tr, b + 1)
                dst = (QT, KTr)[b // 4][:, 2 * (b % 4):2 * (b % 4) + 2, :]
                nc.scalar.activation(dst, PS[:, b, :].rearrange("p (a b) -> p a b", a=2), ACT.Copy).then_inc(qk_out, 1)

            def exps(c):
                act.wait_ge(maxed, c + 1)
                if c >= 2:
                    act.wait_ge(mixed_probs, c - 1)
                keys = P * (c % 2 + 1)
                for m in range(2):
                    ins = nc.scalar.activation(PR[:, c % 2, m, 0:keys], S[:, c % 2, m, 0:keys], ACT.Exp,
                                               bias=NB[:, c % 2, m:m + 1], scale=QK ** -0.5,
                                               accum_out=LS[:, c % 2, m:m + 1])
                ins.then_inc(exped, 1)

            exps(0)
            for c in range(2 * HEADS):
                if c + 1 < 2 * HEADS:
                    exps(c + 1)
                h, tt = divmod(c, 2)
                act.wait_ge(at_done, c + 1)
                nc.scalar.activation(AT[:, c % 2, 0:tt + 1, :],
                                     PS[:, 4 + c % 2, 0:P * (tt + 1)].rearrange("p (a b) -> p a b", b=P),
                                     ACT.Copy).then_inc(at_out, 1)
                act.wait_ge(pv_done, c + 1)
                nc.scalar.activation(MIX[:, tt, h * VD:(h + 1) * VD], PS[:, 6 + c % 2, 0:VD], ACT.Copy).then_inc(pv_out, 1)
            act.wait_ge(sz_read, 16)
            for tt in range(TT):
                squares(MIX[:, tt, HALF:D], tt, JUNK[:, 0:HALF])
            root(3, SS[:, 2:4], SS[:, 2:4])
            root(4, GS[:, 1], GS[:, 1])
            act.wait_ge(used, OUT0)
            transposed_hi(1, None)
            for n in range(OUT0 + 4, WQ0 + 4):
                hi(n, n % 4)
            act.wait_ge(x1_ready, 8)
            for tt in range(TT):
                squares(X[:, tt, :], tt, JUNK[:])
            root(5, SS[:, 2:4], SS[:, 2:4])
            transposed_hi(2, 1)
            for n in range(WQ0 + 4, U0):
                hi(n, n % 4)
            for tt in range(TT):
                for b in range(4):
                    act.wait_ge(sc_done, 4 * tt + b + 1)
                    nc.scalar.activation(SC[:, tt, 4 * b:4 * b + 4, :],
                                         PS[:, 4 + b, :].rearrange("p (a b) -> p a b", b=NKEYS), ACT.Copy).then_inc(sc_out, 1)
            for tt in range(TT):
                act.wait_ge(best_ready, tt + 1)
                nc.scalar.activation(ROWS[:, 2, :], ROWS[:, 2, :], ACT.Exp).then_inc(gexp, 1)
            for tt in range(TT):
                act.wait_ge(picks_tr, tt + 1)
                nc.scalar.activation(EG[:, :, tt * P:(tt + 1) * P],
                                     PS[:, 7 - tt, 0:3 * P].rearrange("p (a b) -> p a b", b=P), ACT.Copy).then_inc(picks_out, 1)

            def gelu(tiles, count):
                act.wait_ge(tile_out, count)
                nc.scalar.activation(tiles, tiles, ACT.Gelu_apprx_tanh).then_inc(gelus, 1)

            for r in range(4):
                hi(U0 + r, r)
            with act.Fori(1, N_U // 4) as i:
                for r in range(4):
                    hi_at(i, 4, U0, r)
                gelu(store[:, bass.ds(i * 2 - 2, 2), :], i * 2 + HC)
            gelu(store[:, NKEYS - 2:NKEYS, :], HC + NKEYS)

            def weight_hi(g, jj, s):
                if jj is not None:
                    act.wait_ge(used, g * 16 + (V0 - 16 + 9 + s))
                nc.scalar.activation(WHL[:, s, 0, :], store[:, bass.ds(g * VG + s, 1), :].rearrange("p a t -> p (a t)"),
                                     ACT.Copy).then_inc(w_hi, 1)

            for u in range(4):
                hi(V0 + u, u)
            act.wait_ge(g_read, T // 4)
            act.wait_ge(g_done, T // 4)
            for s in range(4):
                weight_hi(0, s, s)

            def values(g, first, last):
                for u in range(16):
                    if not (first and u < 4):
                        hi_at(g, 16, V0, u)
                    if u < 4:
                        weight_hi(g, u + 4, u + 4)
                    if u >= 12 and not last:
                        weight_hi(g + 1, u - 12, u - 12)

            values(0, True, False)
            with act.Fori(1, N_VG - 1) as g:
                values(g, False, False)
            values(N_VG - 1, False, True)
            act.wait_ge(flushed, 8 * N_VG)
            for tt in range(TT):
                squares(ACC[:, tt, :], tt, FJ[:])
            root(6, SS[:, 2:4], SS[:, 2:4])

        @block.vector
        def _(dve):
            chain = [0]
            v = nc.vector

            def link(ins):
                chain[0] += 1
                ins.then_inc(dve_chain, 1)
                dve.wait_ge(dve_chain, chain[0])

            def split(s4, s2):
                v.tensor_tensor(LO[:, s2, :], RAW[:, s4, :], HI[:, s4, :].bitcast(FP32), ALU.subtract).then_inc(lo_ready, 1)

            def lo(n):
                dve.wait_ge(hi_ready, n + 1)
                if n >= LO_SLOTS:
                    dve.wait_ge(used, n - (LO_SLOTS - 1))
                split(n % 4, n % 2)

            def lo_at(it, per, first, u):
                dve.wait_ge(hi_ready, it * per + (first + u + 1))
                dve.wait_ge(used, it * per + (first + u - (LO_SLOTS - 1)))
                split(u % 4, u % 2)

            def mean(dst, src, n):
                v.tensor_scalar(dst, src, 1.0 / n, EPS, ALU.mult, ALU.add).then_inc(means, 1)

            def transposed_lo(rnd, gain):
                for kp in range(KT // 2):
                    dve.wait_ge(tr_hi, 8 * rnd + kp + 1)
                    for k in (2 * kp, 2 * kp + 1):
                        src = PS[:, kp, (k % 2) * T:(k % 2 + 1) * T]
                        hi_part = xT[:, k, 0, :].bitcast(FP32)
                        if gain is None:
                            ins = v.tensor_tensor(xT[:, k, 1, :], src, hi_part, ALU.subtract)
                        else:
                            ins = v.scalar_tensor_tensor(xT[:, k, 1, :], src, GT[:, gain, k:k + 1], hi_part,
                                                         ALU.mult, ALU.subtract)
                    ins.then_inc(tr_lo, 1)

            def norm_rows(n_root, n_sums):
                dve.wait_ge(sums, n_sums)
                mean(SS[:, 2:4], SS[:, 0:2], D)
                dve.wait_ge(roots, n_root)
                link(v.reciprocal(SS[:, 4:6], SS[:, 2:4]))
                for tt in range(TT):
                    v.tensor_scalar(XS[:, tt, :], X[:, tt, :], SS[:, 4 + tt:5 + tt], None, ALU.mult).then_inc(rows_ready, 1)

            for n in range(2):
                lo(n)
            norm_rows(1, 2)
            transposed_lo(0, 0)

            def group_sums(rows):
                for tt in range(TT):
                    link(v.tensor_tensor(SQ[:, tt, :], rows(tt), rows(tt), ALU.mult))
                    link(v.tensor_reduce(GS[:, 0, tt, :], SQ[:, tt, :].rearrange("p (a b) -> p a b", b=P), AX.X, ALU.add))
                mean(GS[:, 1], GS[:, 0], P)

            def group_scale(rows, gain):
                link(v.reciprocal(GS[:, 2], GS[:, 1]))
                for tt in range(TT):
                    by = rows(tt).rearrange("p (a b) -> p a b", b=P)
                    link(v.tensor_tensor(by, by, GS[:, 2, tt, :].unsqueeze(2).broadcast_to([P, 8, P]), ALU.mult))
                    ins = v.tensor_tensor(by, by, gain, ALU.mult)
                return ins

            for n in range(2, N_PROJ + 2):
                lo(n)
                if n == KT + 8:
                    dve.wait_ge(evac, 4)
                    group_sums(lambda tt: GRP[:, Z_, tt, :])
                if n == 2 * KT + 12:
                    dve.wait_ge(roots, 2)
                    group_scale(lambda tt: GRP[:, Z_, tt, :], ZG[:].rearrange("p (a b) -> p a b", b=P)).then_inc(z_ready, 1)
            dve.wait_ge(evac, 16)
            for tt in range(TT):
                qk = GRP[:, Q_:K_ + 1, tt, :].rearrange("p a (b d) -> p a b d", d=QK)
                lo_half, hi_half = qk[:, :, :, 0:ROT], qk[:, :, :, ROT:2 * ROT]

                def table(which):
                    return ROPE[:, which, tt, :].unsqueeze(1).unsqueeze(1).broadcast_to([P, 2, 16, ROT])

                r4 = [RT[:, i].rearrange("p (a b) d -> p a b d", a=2) for i in range(4)]
                v.tensor_tensor(r4[0], lo_half, table(0), ALU.mult)
                v.tensor_tensor(r4[1], hi_half, table(1), ALU.mult)
                v.tensor_tensor(r4[2], hi_half, table(0), ALU.mult)
                link(v.tensor_tensor(r4[3], lo_half, table(1), ALU.mult))
                v.tensor_tensor(lo_half, r4[0], r4[1], ALU.subtract)
                link(v.tensor_tensor(hi_half, r4[2], r4[3], ALU.add))
            v.engine_nop().then_inc(roped, 1)
            link(v.tensor_tensor(SQ[:, 0, 0:2 * QK].rearrange("p (a b) -> p a b", a=2), LAMV[:, 0:4:2, :], LAMV[:, 1:4:2, :],
                                 ALU.mult))
            v.tensor_reduce(LAM[:, 0:2], SQ[:, 0, 0:2 * QK].rearrange("p (a b) -> p a b", a=2), AX.X, ALU.add)\
                .then_inc(lam_sums, 1)
            for tt in range(TT):
                for g in range(GROUPS):
                    dve.wait_ge(sz_done, 2 * tt + g // 4 + 1)
                    cols = slice(g * P, (g + 1) * P)
                    v.scalar_tensor_tensor(MIX[:, tt, HALF + g * P:HALF + (g + 1) * P],
                                           PS[:, 4 + 2 * tt + g // 4, (g % 4) * P:(g % 4 + 1) * P],
                                           BS[:, g:g + 1], GRP[:, U_, tt, cols], ALU.add, ALU.mult).then_inc(sz_read, 1)
            dve.wait_ge(lam_exp, 1)
            link(v.tensor_tensor(LAM[:, 4:5], LAM[:, 3:4], LAM[:, 2:3], ALU.subtract))
            link(v.tensor_scalar(LAM[:, 5:6], LAM[:, 4:5], -LAMBDA_INIT, None, ALU.add))

            def shift_max(c):
                tt = c % 2
                keys = P * (tt + 1)
                dve.wait_ge(scored, c + 1)
                if c >= 2:
                    dve.wait_ge(exped, c - 1)
                link(v.tensor_tensor(S[:, c % 2, :, 0:keys], PS[:, 2 * (c % 2):2 * (c % 2) + 2, 0:keys],
                                     MASK[:, tt, 0:keys].unsqueeze(1).broadcast_to([P, 2, keys]), ALU.add))
                link(v.tensor_reduce(RL[:, c % 2, :], S[:, c % 2, :, 0:keys], AX.X, ALU.max))
                v.tensor_scalar(NB[:, c % 2, :], RL[:, c % 2, :], -(QK ** -0.5), None, ALU.mult).then_inc(maxed, 1)

            shift_max(0)
            for c in range(2 * HEADS):
                if c + 1 < 2 * HEADS:
                    shift_max(c + 1)
                keys = P * (c % 2 + 1)
                dve.wait_ge(exped, c + 1)
                if c >= 2:
                    dve.wait_ge(at_done, c - 1)
                link(v.reciprocal(RL[:, c % 2, :], LS[:, c % 2, :]))
                link(v.tensor_tensor(RL[:, c % 2, 1:2], RL[:, c % 2, 1:2], LAM[:, 5:6], ALU.mult))
                link(v.tensor_scalar(PR[:, c % 2, 1, 0:keys], PR[:, c % 2, 1, 0:keys], RL[:, c % 2, 1:2], None, ALU.mult))
                v.scalar_tensor_tensor(AM[:, c % 2, 0:keys], PR[:, c % 2, 0, 0:keys], RL[:, c % 2, 0:1],
                                       PR[:, c % 2, 1, 0:keys], ALU.mult, ALU.add).then_inc(mixed_probs, 1)
            dve.wait_ge(sums, 4)
            mean(SS[:, 2:4], SS[:, 0:2], HALF)
            dve.wait_ge(pv_out, 16)
            dve.wait_ge(roots, 3)
            group_sums(lambda tt: MIX[:, tt, 0:HALF])
            link(v.tensor_scalar(SG[:], SG[:], 1.0 - LAMBDA_INIT, None, ALU.mult))
            link(v.reciprocal(SS[:, 4:6], SS[:, 2:4]))
            for tt in range(TT):
                v.scalar_tensor_tensor(MIX[:, tt, HALF:D], MIX[:, tt, HALF:D], SS[:, 4 + tt:5 + tt], OG[:],
                                       ALU.mult, ALU.mult)
            dve.wait_ge(roots, 4)
            group_scale(lambda tt: MIX[:, tt, 0:HALF], SG[:].unsqueeze(1).broadcast_to([P, HEADS, VD])).then_inc(rows_ready, 2)
            transposed_lo(1, None)
            for n in range(OUT0 + 2, WQ0 + 2):
                lo(n)
            for g in range(2):
                for tt in range(TT):
                    for c in range(2):
                        cols = slice(g * UNIT + c * BANK, g * UNIT + (c + 1) * BANK)
                        v.tensor_tensor(X[:, tt, cols], PS[:, 4 * g + 2 * tt + c, :], X[:, tt, cols], ALU.add)\
                            .then_inc(x1_ready, 1)
            norm_rows(5, 6)
            transposed_lo(2, 1)

            def add_halves(dst, bank):
                return v.tensor_reduce(dst, PS[:, bank, :].rearrange("p (a t) -> p t a", a=2), AX.X, ALU.add)

            def query(c):
                dve.wait_ge(used, WQ0 + 2 * c + 2)
                add_halves(QTQ[:, c, :], c % 2).then_inc(tile_out, 1)

            for n in range(WQ0 + 2, U0):
                lo(n)
                if n % 2 and n >= WQ0 + 3:
                    query((n - WQ0 - 3) // 2)
            query(HC - 1)

            for tt in range(TT):
                for c in range(HC):
                    dve.wait_ge(sc_out, 4 * tt + c // 4 + 1)
                    row = SC[:, tt, c, :]
                    for r in range(2):
                        best = S16[:, tt, c, 8 * r:8 * r + 8]
                        link(v.max(best, row))
                        v.max_index(I16[:, tt, c, 8 * r:8 * r + 8], best, row)
                        if r == 0:
                            link(v.match_replace(row, best, row, FLOOR))
            for tt in range(TT):
                link(v.tensor_copy(I16F[:, tt], I16[:, tt]))
                s1, s2 = S16[:, tt, 0:HC:2, :], S16[:, tt, 1:HC:2, :]
                i1, i2 = I16F[:, tt, 0:HC:2, :], I16F[:, tt, 1:HC:2, :]
                grid = [P, PH, TOPK, TOPK]
                link(v.tensor_tensor(CAND[:], s1.unsqueeze(3).broadcast_to(grid), s2.unsqueeze(2).broadcast_to(grid), ALU.add))
                for h in range(PH):
                    row = CAND[:, h].rearrange("p a b -> p (a b)")
                    for r in range(2):
                        best = BEST[:, h, 8 * r:8 * r + 8]
                        link(v.max(best, row))
                        v.max_index(CI[:, h, 8 * r:8 * r + 8], best, row)
                        if r == 0:
                            link(v.match_replace(row, best, row, FLOOR))
                if tt:
                    dve.wait_ge(picks_tr, 1)
                v.tensor_tensor(ROWS[:, 2].rearrange("p (h k) -> p h k", h=PH), BEST[:],
                                BEST[:, :, 0:1].broadcast_to([P, PH, TOPK]), ALU.subtract).then_inc(best_ready, 1)
                dve.wait_ge(best_ready, tt + 1)
                for half, (op, by, lst) in enumerate(((ALU.logical_shift_right, 4, i1), (ALU.bitwise_and, 15, i2))):
                    link(v.tensor_scalar(CIA[:], CI[:], by, None, op))
                    link(v.tensor_copy(CF[:], CIA[:]))
                    link(v.tensor_tensor(EQ[:], CF[:].unsqueeze(3).broadcast_to(grid),
                                         IOTA[:, 0:TOPK].unsqueeze(1).unsqueeze(1).broadcast_to(grid), ALU.is_equal))
                    link(v.tensor_tensor(EQ[:], EQ[:], lst.unsqueeze(2).broadcast_to(grid), ALU.mult))
                    link(v.tensor_reduce(ROWS[:, half].rearrange("p (h k) -> p h k", h=PH), EQ[:], AX.X, ALU.add))
                dve.wait_ge(gexp, tt + 1)
                gates = ROWS[:, 2].rearrange("p (h k) -> p h k", h=PH)
                link(v.tensor_reduce(GM[:, 0, :], gates, AX.X, ALU.add))
                link(v.reciprocal(GM[:, 1, :], GM[:, 0, :]))
                v.tensor_tensor(gates, gates, GM[:, 1, :].unsqueeze(2).broadcast_to([P, PH, TOPK]), ALU.mult).then_inc(picks, 1)

            def score(it, j, r, units):
                dve.wait_ge(used, units)
                add_halves(store[:, bass.ds(j, 1), :].rearrange("p a t -> p (a t)"), r).then_inc(tile_out, 1)

            for n in range(U0, U0 + 4):
                lo(n)
            dve.wait_ge(x1_saved, 16 * TT)
            score(0, 0, 0, U0 + 2)
            with dve.Fori(1, N_U // 4) as i:
                for r in range(4):
                    lo_at(i, 4, U0, r)
                    if r == 1:
                        score(i, i * 2 - 1, 1, i * 4 + U0)
                    if r == 3:
                        score(i, i * 2, 0, i * 4 + (U0 + 2))
            score(0, NKEYS - 1, 1, V0)

            for u in range(2):
                lo(V0 + u)
            dve.wait_ge(gelus, N_U // 4)
            dve.wait_ge(picks_out, TT)

            def one_hot(i, s):
                for dst, row, signal in ((ONE1, 0, one1), (ONE2, 1, one2)):
                    v.tensor_tensor(dst[:, s], IOTA[:].unsqueeze(1).broadcast_to([P, TOK8, NKEYS]),
                                    EG[:, row, bass.ds(i * 16 + 8 * s, TOK8)].unsqueeze(2).broadcast_to([P, TOK8, NKEYS]),
                                    ALU.is_equal).then_inc(signal, 1)

            def gate(i, b):
                dve.wait_ge(g_done, i * 4 + (b + 1))
                part = store[:, :, bass.ds(i * 16 + 4 * b, 4)]
                v.tensor_tensor(part, part, PS[:, b, :].rearrange("p (t j) -> p j t", t=4), ALU.mult).then_inc(g_read, 1)

            for s in range(2):
                one_hot(0, s)
            with dve.Fori(1, T // 16) as i:
                for s in range(2):
                    for b in (2 * s, 2 * s + 1):
                        gate(i - 1, b)
                    dve.wait_ge(g_done, i * 4 + (2 * s - 2))
                    one_hot(i, s)
            for b in range(4):
                gate(T // 16 - 1, b)

            def weight_lo(g, s):
                dve.wait_ge(w_hi, g * VG + (s + 1))
                v.tensor_tensor(WHL[:, s, 1, :], store[:, bass.ds(g * VG + s, 1), :].rearrange("p a t -> p (a t)"),
                                WHL[:, s, 0, :].bitcast(FP32), ALU.subtract).then_inc(w_lo, 1)

            def flush(g, h, b, peeled):
                dve.wait_ge(used, g * 16 + (V0 + 8 * h + 8))
                tt, c = divmod(b, 2)
                cols = slice(h * UNIT + c * BANK, h * UNIT + (c + 1) * BANK)
                if not peeled:
                    dve.wait_ge(flushed, g * 8 + (4 * h + b - 7))
                v.tensor_tensor(ACC[:, tt, cols], PS[:, 4 * h + b, :], ACC[:, tt, cols], ALU.add).then_inc(flushed, 1)

            def values(g, first, second):
                for u in range(16):
                    if not (first and u < 2):
                        lo_at(g, 16, V0, u)
                    if u < 4:
                        weight_lo(g, u + 4)
                    if u >= 12 and not (isinstance(g, int) and g == N_VG - 1):
                        weight_lo(g + 1, u - 12)
                    if 1 <= u <= 4 and not first:
                        flush(g - 1, 1, u - 1, second)
                    if 9 <= u <= 12:
                        flush(g, 0, u - 9, first)

            for s in range(4):
                weight_lo(0, s)
            dve.wait_ge(x1_back, 16 * TT)
            values(0, True, False)
            values(1, False, True)
            with dve.Fori(2, N_VG - 1) as g:
                values(g, False, False)
            values(N_VG - 1, False, False)
            for b in range(4):
                flush(N_VG - 1, 1, b, False)
            dve.wait_ge(sums, 8)
            mean(SS[:, 2:4], SS[:, 0:2], D)
            dve.wait_ge(roots, 6)
            dve.wait_ge(fg_ready, 16)
            link(v.reciprocal(SS[:, 4:6], SS[:, 2:4]))
            for tt in range(TT):
                v.scalar_tensor_tensor(ACC[:, tt, :], ACC[:, tt, :], SS[:, 4 + tt:5 + tt], FG[:],
                                       ALU.mult, ALU.mult).then_inc(fin, 1)

        @block.tensor
        def _(pe):
            mm = nc.tensor.matmul

            def transpose_rows(rnd, src):
                pe.wait_ge(rows_ready, 2 * rnd + 2)
                for kp in range(KT // 2):
                    for k in (2 * kp, 2 * kp + 1):
                        for tt in range(TT):
                            last = nc.tensor.transpose(PS[:, kp, (k % 2) * T + tt * P:(k % 2) * T + (tt + 1) * P],
                                                       src[:, tt, k * P:(k + 1) * P], IDENT[:])
                    last.then_inc(tr_done, 1)

            def row_unit(u, bank, high, low, first, last):
                h, l = HI[:, u % 4, :], LO[:, u % 2, :]
                for tt in range(TT):
                    for c in range(2):
                        cols = slice(c * BANK, (c + 1) * BANK)
                        mm(PS[:, bank + 2 * tt + c, :], high(tt), h[:, cols], start=first, stop=False)
                        mm(PS[:, bank + 2 * tt + c, :], high(tt), l[:, cols], start=False, stop=False)
                    for c in range(2):
                        cols = slice(c * BANK, (c + 1) * BANK)
                        ins = mm(PS[:, bank + 2 * tt + c, :], low(tt), h[:, cols], start=False, stop=last)
                ins.then_inc(used, 1)

            def column_unit(u, bank):
                half = u % 2
                for kk in range(KT // 2):
                    k = (KT // 2) * half + kk
                    cols = slice(kk * P, (kk + 1) * P)
                    if kk:
                        mm(PS[:, bank, 0:T], LO[:, u % 2, cols], xT[:, k, 0, :], start=False, stop=False)
                    ins = mm(PS[:, bank, :], HI[:, u % 4, cols], xT[:, k].rearrange("p a t -> p (a t)"),
                             start=k == 0, stop=k == KT - 1)
                    if not kk:
                        ins = mm(PS[:, bank, 0:T], LO[:, u % 2, cols], xT[:, k, 0, :], start=False, stop=False)
                ins.then_inc(used, 1)

            def x_part(k, part):
                return lambda tt: xT[:, k, part, tt * P:(tt + 1) * P]

            pe.wait_ge(consts, 4)
            transpose_rows(0, XS)
            pe.wait_ge(tr_lo, 8)
            for g in range(5):
                if g >= 2:
                    pe.wait_ge(evac, 4 * (g - 1))
                for k in range(KT):
                    n = g * KT + k
                    pe.wait_ge(lo_ready, n + 1)
                    row_unit(n, 4 * (g % 2), x_part(k, 0), x_part(k, 1), k == 0, k == KT - 1)
            pe.wait_ge(z_ready, 1)
            pe.wait_ge(consts, 8)
            pe.wait_ge(evac, 16)
            for tt in range(TT):
                for g in range(GROUPS):
                    last = mm(PS[:, 4 + 2 * tt + g // 4, (g % 4) * P:(g % 4 + 1) * P], WST[:, g, :],
                              GRP[:, Z_, tt, g * P:(g + 1) * P], start=True, stop=True)
                    if g % 4 == 3:
                        last.then_inc(sz_done, 1)
            pe.wait_ge(roped, 1)
            pe.wait_ge(evac, 20)
            for b in range(8):
                if b == 4:
                    pe.wait_ge(sz_read, 16)
                for h in (2 * (b % 4), 2 * (b % 4) + 1):
                    for tt in range(TT):
                        last = nc.tensor.transpose(PS[:, b, (h % 2) * T + tt * P:(h % 2) * T + (tt + 1) * P],
                                                   GRP[:, (Q_, K_)[b // 4], tt, h * P:(h + 1) * P], IDENT[:])
                last.then_inc(qk_tr, 1)
            pe.wait_ge(qk_out, 8)

            def scores(c):
                h, tt = divmod(c, 2)
                keys = P * (tt + 1)
                if c >= 2:
                    pe.wait_ge(maxed, c - 1)
                for m in range(2):
                    half = slice(QK * m, QK * (m + 1))
                    last = mm(PS[:, 2 * (c % 2) + m, 0:keys], QT[half, h, tt * P:(tt + 1) * P], KTr[half, h, 0:keys],
                              start=True, stop=True)
                last.then_inc(scored, 1)

            scores(0)
            for c in range(2 * HEADS):
                if c + 1 < 2 * HEADS:
                    scores(c + 1)
                h, tt = divmod(c, 2)
                pe.wait_ge(mixed_probs, c + 1)
                if c >= 2:
                    pe.wait_ge(at_out, c - 1)
                for kt in range(tt + 1):
                    last = nc.tensor.transpose(PS[:, 4 + c % 2, kt * P:(kt + 1) * P], AM[:, c % 2, kt * P:(kt + 1) * P], IDENT[:])
                last.then_inc(at_done, 1)
                pe.wait_ge(at_out, c + 1)
                if c >= 2:
                    pe.wait_ge(pv_out, c - 1)
                for kt in range(tt + 1):
                    last = mm(PS[:, 6 + c % 2, 0:VD], AT[:, c % 2, kt, :], GRP[:, V_, kt, h * VD:(h + 1) * VD],
                              start=kt == 0, stop=kt == tt)
                last.then_inc(pv_done, 1)
            pe.wait_ge(pv_out, 16)
            transpose_rows(1, MIX)
            pe.wait_ge(tr_lo, 16)
            for g in range(2):
                for k in range(KT):
                    n = OUT0 + g * KT + k
                    pe.wait_ge(lo_ready, n + 1)
                    row_unit(n, 4 * g, x_part(k, 0), x_part(k, 1), k == 0, k == KT - 1)
            pe.wait_ge(x1_ready, 8)
            transpose_rows(2, XS)
            pe.wait_ge(tr_lo, 24)
            for u in range(N_WQ):
                pe.wait_ge(lo_ready, WQ0 + u + 1)
                if u % 2 == 0 and u >= 4:
                    pe.wait_ge(tile_out, u // 2 - 1)
                column_unit(u, (u // 2) % 2)
            pe.wait_ge(tile_out, HC)
            pe.wait_ge(keys_ready, 16)
            for tt in range(TT):
                for b in range(4):
                    if tt:
                        pe.wait_ge(sc_out, b + 1)
                    for c in range(4 * b, 4 * b + 4):
                        last = mm(PS[:, 4 + b, (c % 4) * NKEYS:(c % 4 + 1) * NKEYS], QTQ[:, c, tt * P:(tt + 1) * P],
                                  KEYS[:, c, :], start=True, stop=True)
                    last.then_inc(sc_done, 1)
            pe.wait_ge(sc_out, 8)
            for tt in range(TT):
                pe.wait_ge(picks, tt + 1)
                for r in range(3):
                    last = nc.tensor.transpose(PS[:, 7 - tt, r * P:(r + 1) * P], ROWS[:, r, :], IDENT[:])
                last.then_inc(picks_tr, 1)
            with pe.Fori(0, N_U // 4) as i:
                for r in range(4):
                    pe.wait_ge(lo_ready, i * 4 + (U0 + r + 1))
                    if r % 2 == 0:
                        pe.wait_ge(tile_out, i * 2 + (HC + r // 2 - 1))
                    column_unit(r, r // 2)
            pe.wait_ge(tile_out, HC + NKEYS)
            with pe.Fori(0, T // 16) as i:
                for s in range(2):
                    pe.wait_ge(one1, i * 2 + (s + 1))
                    pe.wait_ge(one2g, i * 2 + (s + 1))
                    for b in (2 * s, 2 * s + 1):
                        pe.wait_ge(one1, i * 2 + (s + 1))
                        for t in range(4):
                            last = mm(PS[:, b, t * NKEYS:(t + 1) * NKEYS], ONE1[:, s, 4 * (b % 2) + t, :],
                                      ONE2[:, s, 4 * (b % 2) + t, :], start=True, stop=True)
                        last.then_inc(g_done, 1)

            def values(g, first):
                for u in range(16):
                    h, jj = divmod(u, VG)
                    pe.wait_ge(lo_ready, g * 16 + (V0 + u + 1))
                    if h == 0:
                        pe.wait_ge(w_lo, g * VG + (jj + 1))
                    if jj == 0 and not first:
                        pe.wait_ge(flushed, g * 8 + (4 * h - 4))
                    row_unit(u, 4 * h, lambda tt: WHL[:, jj, 0, tt * P:(tt + 1) * P],
                             lambda tt: WHL[:, jj, 1, tt * P:(tt + 1) * P], jj == 0, jj == VG - 1)

            pe.wait_ge(g_read, T // 4)
            values(0, True)
            with pe.Fori(1, N_VG) as g:
                values(g, False)


def kernel(**inputs):
    import concourse.bacc as bacc
    from concourse.bass_utils import run_bass_kernel_spmd

    a = {k: np.asarray(w) for k, w in inputs.items()}
    inv = (500000.0 ** (-np.arange(0, 2 * ROT, 2, dtype=np.float32) / np.float32(2 * ROT))).astype(np.float32)
    ang = np.arange(T, dtype=np.float32)[:, None] * inv[None, :]
    rope = np.stack([np.cos(ang), np.sin(ang)]).astype(np.float32)
    arrays = {
        "x": a["x"].reshape(T, D),
        "w_in": a["w_in"][0],
        "w_out": a["w_out"][0],
        "wq_t": a["peer_w_q"][0].reshape(KT, P, HC, P).transpose(2, 1, 0, 3).reshape(HC, P, D),
        "keys_t": a["peer_sub_keys"][0].transpose(3, 0, 1, 2).reshape(P, HC, NKEYS),
        "u_t": a["peer_u"][0].reshape(NKEYS, NKEYS, KT, P).transpose(1, 3, 2, 0).reshape(NKEYS, P, D),
        "peer_v": a["peer_v"][0],
        "ws_t": a["gmlp_w_s"][0].transpose(2, 0, 1),
        "bs_t": a["gmlp_b_s"][0].T,
        "gain_t": np.stack([a["mix_norm_g"][0].reshape(KT, P), a["ffn_norm_g"][0].reshape(KT, P)]).transpose(2, 0, 1),
        "z_gain": a["gmlp_z_norm_g"].reshape(1, HALF),
        "out_gain": a["gmlp_out_g"].reshape(1, HALF),
        "subln_gain": a["subln_g"].reshape(1, VD),
        "final_gain": a["final_norm_g"].reshape(1, D),
        "lambdas": np.concatenate([a["lambda_q1"], a["lambda_k1"], a["lambda_q2"], a["lambda_k2"]], axis=1),
        "rope": rope.reshape(2, TT, P, ROT).transpose(2, 0, 1, 3),
    }
    arrays = {k: np.ascontiguousarray(w) for k, w in arrays.items()}
    nc = bacc.Bacc("TRN2", target_bir_lowering=False, num_devices=1)
    args = [nc.dram_tensor(k, w.shape, mybir.dt.from_np(w.dtype), kind="ExternalInput").ap() for k, w in arrays.items()]
    out = nc.dram_tensor("out", [T, D], FP32, kind="ExternalOutput").ap()
    hybrid_peer_block(nc, *args, out)
    got = run_bass_kernel_spmd(nc, [arrays], core_ids=[0]).results[0]["out"]
    return got.reshape(1, T, D)
```

```python
import math

import numpy as np
import concourse.bass as bass
from concourse import mybir
from contextlib import ExitStack

FP32 = mybir.dt.float32
FP32R = mybir.dt.float32r
U32 = mybir.dt.uint32
ALU = mybir.AluOpType
ACT = mybir.ActivationFunctionType
AX = mybir.AxisListType

P = 128
T, D = 256, 2048
TT = T // P
KT = D // P
HALF = D // 2
BANK = 512
HEADS, QK, VD = 8, 64, 128
ROT = 8
CHUNK = 64
GROUPS = 8
EPS = 1e-6
LAMBDA_INIT = 0.8 - 0.6 * math.exp(-0.3 * 0)
PH, TOPK, NKEYS = 8, 16, 128
HC = 2 * PH
FLOOR = -3.0e38
NEG = -1e30

UNIT = 1024
N_PROJ, N_OUT, N_WQ, N_U, N_V = 5 * KT, 2 * KT, 2 * HC, 2 * NKEYS, 2 * NKEYS
OUT0 = N_PROJ
WQ0 = OUT0 + N_OUT
U0 = WQ0 + N_WQ
V0 = U0 + N_U
END = V0 + N_V
RAW_SLOTS, HI_SLOTS, LO_SLOTS = 4, 4, 2
VG = 8
N_VG = NKEYS // VG
Q_, K_, V_, Z_, U_ = range(5)
COLS = {Z_: 4096, U_: 3072, Q_: 0, K_: 1024, V_: 2048}
ATT0 = 3 * KT
COMBOS = TT * HEADS
BESIDE0, BESIDE1 = ATT0, ATT0 + 2 * KT
TOK8 = 8
PIECES = HC + 2 + PH + 2 * 7 + 1
PICKS_AT = (14, 24)
GATES_AT = (10, 20)
BANK0 = (0, 4, 0, 4, 4)
SPREAD_U = (2, 4, 6, 10)
E2A = 64
PAIRS = NKEYS // 2
SPREAD1 = 32
N_B = 28
B_ALL = T // TOK8
B2 = 4


def hybrid_peer_block(nc, x, w_in, w_out, wq_t, keys_t, u_t, peer_v, ws_t, bs_t, gain_t, z_gain, out_gain,
                      subln_gain, final_gain, lambdas, rope, out):
    ctx = ExitStack()
    with ctx:
        base = (nc.sbuf_base + 63) // 64 * 64

        def at(name, off, shape, dt=FP32):
            return nc.alloc_sbuf_tensor_at(name, shape, dt, offset=base + off)

        def sem(name):
            return ctx.enter_context(nc.semaphore(name))

        KB = 1024
        store = at("store", 0, [P, NKEYS, T])
        X = at("X", 0, [P, TT, D])
        GRP = at("GRP", 16 * KB, [P, 5, TT, HALF])
        MIX = at("MIX", 56 * KB, [P, TT, D])
        QT = at("QT", 72 * KB, [P, HEADS, T])
        KTr = at("KTr", 80 * KB, [P, HEADS, T])
        PR = at("PR", 88 * KB, [P, 2, 2, T])
        AM = at("AM", 92 * KB, [P, 2, T])
        AT = at("AT", 94 * KB, [P, 2, P])
        XS = at("XS", 72 * KB, [P, TT, D])
        SQ = at("SQ", 96 * KB, [P, HALF])
        JUNK = at("JUNK", 100 * KB, [P, HALF])
        RT = at("RT", 104 * KB, [P, 4, 2 * HEADS, ROT])
        SQX = at("SQX", 88 * KB, [P, TT, D])
        ZG = at("ZG", 110 * KB, [P, HALF])
        OG = at("OG", 114 * KB, [P, HALF])
        WST = at("WST", 118 * KB, [P, GROUPS, P])
        SG = at("SG", 122 * KB, [P, VD])
        LAMV = at("LAMV", 123 * KB, [P, 4, QK])
        ROPE = at("ROPE", 124 * KB, [P, 2, TT, ROT])
        SC = at("SC", 64 * KB, [P, TT, HC, NKEYS])
        QTQ = at("QTQ", 80 * KB, [P, HC, T])
        KEYS = at("KEYS", 96 * KB, [P, HC, NKEYS])
        CAND = at("CAND", 104 * KB, [P, PH, TOPK, TOPK])
        EQ = at("EQ", 112 * KB, [P, PH, TOPK, TOPK])
        S16 = at("S16", 120 * KB, [P, TT, HC, TOPK])
        I16 = at("I16", 122 * KB, [P, TT, HC, TOPK], U32)
        I16F = at("I16F", 124 * KB, [P, TT, HC, TOPK])
        BEST = at("BEST", 126 * KB, [P, PH, TOPK])
        CI = at("CI", 126 * KB + 512, [P, PH, TOPK], U32)
        CIA = at("CIA", 127 * KB, [P, PH, TOPK], U32)
        CF = at("CF", 127 * KB + 512, [P, PH, TOPK])
        ROWS = at("ROWS", 62 * KB, [P, 3, PH * TOPK])
        xT = at("xT", 128 * KB, [P, KT, 2, T], FP32R)
        ACC = at("ACC", 128 * KB, [P, TT, D])
        WHL = at("WHL", 144 * KB, [P, VG, 2, T], FP32R)
        ONES = [(at("ONE1A", 122 * KB, [P, TOK8, NKEYS]), at("ONE2A", 126 * KB, [P, TOK8, E2A])),
                (at("ONE1B", 144 * KB, [P, 2, TOK8, NKEYS]), at("ONE2B", 152 * KB, [P, 2, TOK8, NKEYS])),
                (at("ONE1C", 0, [P, TOK8, NKEYS]), at("ONE2C", 4 * KB, [P, TOK8, E2A]))]
        FG = at("FG", 0, [P, D])
        FJ = at("FJ", 8 * KB, [P, HALF])
        RAW = at("RAW", 160 * KB, [P, RAW_SLOTS, UNIT])
        HI = at("HI", 176 * KB, [P, HI_SLOTS, UNIT], FP32R)
        LO = at("LO", 192 * KB, [P, LO_SLOTS, UNIT], FP32R)
        off = [200 * KB]

        def small(name, shape, dt=FP32):
            n = 4 * int(np.prod(shape[1:]))
            t = at(name, off[0], shape, dt)
            off[0] += (n + 31) // 32 * 32
            return t

        IDENT = small("IDENT", [P, P])
        IOTA = small("IOTA", [P, NKEYS])
        EG = small("EG", [P, 3, T])
        GT = small("GT", [P, 2, KT])
        BS = small("BS", [P, GROUPS])
        SS = small("SS", [P, 10])
        GS = small("GS", [P, 2, 3, TT, GROUPS])
        LAM = small("LAM", [P, 8])
        NB = small("NB", [P, 2, 2])
        LS = small("LS", [P, 2, 2])
        RL = small("RL", [P, 2, 2])
        GM = small("GM", [P, 3, PH])

        PS = ctx.enter_context(nc.psum_tensor("PS", [P, 8, BANK], FP32))
        x1_dram = nc.dram_tensor("x1_spill", [T, D], FP32).ap()

        raw_ready = [sem(f"raw_ready{i}") for i in range(RAW_SLOTS)]
        hi_ready, used = sem("hi_ready"), sem("used")
        lo_ready = [sem(f"lo_ready{i}") for i in range(LO_SLOTS)]
        x_ready, small_ready = [sem(f"x_ready{i}") for i in range(TT)], sem("small_ready")
        consts = sem("consts")
        dve_chain = sem("dve_chain")
        sums0 = sem("sums0")
        sums = sem("sums")
        means = sem("means")
        roots = sem("roots")
        rows_ready = sem("rows_ready")
        tr_done, tr_hi, tr_lo = sem("tr_done"), sem("tr_hi"), sem("tr_lo")
        evac = sem("evac")
        z_ready, sz_done, sz_read = sem("z_ready"), sem("sz_done"), sem("sz_read")
        roped, qk_tr, qk_out = sem("roped"), sem("qk_tr"), sem("qk_out")
        scored, maxed, exped = sem("scored"), sem("maxed"), sem("exped")
        lam_sums, lam_exp, mixed_probs = sem("lam_sums"), sem("lam_exp"), sem("mixed_probs")
        heads_ready = sem("heads_ready")
        at_done, at_out, pv_done, pv_out = sem("at_done"), sem("at_out"), sem("pv_done"), sem("pv_out")
        x1_ready, x1_saved, x1_back = sem("x1_ready"), sem("x1_saved"), sem("x1_back")
        tile_out = sem("tile_out")
        keys_ready = sem("keys_ready")
        sc_done, sc_out = sem("sc_done"), sem("sc_out")
        best_ready, gexp = sem("best_ready"), sem("gexp")
        picks, picks_tr, picks_out = sem("picks"), sem("picks_tr"), sem("picks_out")
        gelus = sem("gelus")
        one1, one2, one2g, g_done, g_read = sem("one1"), sem("one2"), sem("one2g"), sem("g_done"), sem("g_read")
        w_hi, w_lo, flushed = sem("w_hi"), sem("w_lo"), sem("flushed")
        scaled, act_scaled = sem("scaled"), sem("act_scaled")
        fg_ready, fin, stored = sem("fg_ready"), sem("fin"), sem("stored")

        v_view = peer_v.rearrange("(e j) d -> e j d", j=NKEYS)
        N_SMALL = 10

        block = ctx.enter_context(nc.Block())

        @block.sync
        def _(sp):
            def former(slot, count):
                sp.wait_ge(lo_ready[slot % 2], count)

            def load(n, slot, src):
                if n is not None and n >= RAW_SLOTS:
                    former(slot, n // 2 - 1)
                sp.dma_start(RAW[:, slot, :], src).then_inc(raw_ready[slot], 16)

            for g in range(5):
                for k in range(KT):
                    n = g * KT + k
                    load(n, n % RAW_SLOTS, w_in[k * P:(k + 1) * P, COLS[g]:COLS[g] + UNIT])
            for g in range(2):
                for k in range(KT):
                    n = OUT0 + g * KT + k
                    load(n, n % RAW_SLOTS, w_out[k * P:(k + 1) * P, g * UNIT:(g + 1) * UNIT])
            for u in range(N_WQ):
                load(WQ0 + u, u % RAW_SLOTS, wq_t[u // 2, :, (u % 2) * UNIT:(u % 2 + 1) * UNIT])
            with sp.Fori(0, N_U // 4) as i:
                for r in range(4):
                    former(r, i * 2 + ((U0 + r) // 2 - 1))
                    load(None, r,
                         u_t[bass.ds(i * 2 + r // 2, 1), :, (r % 2) * UNIT:(r % 2 + 1) * UNIT]
                         .rearrange("a p n -> p (a n)"))
            with sp.Fori(0, N_VG) as g:
                for u in range(2 * VG):
                    h, jj = divmod(u, VG)
                    former(u, g * VG + ((V0 + u) // 2 - 1))
                    load(None, u % RAW_SLOTS,
                         v_view[:, bass.ds(g * VG + jj, 1), h * UNIT:(h + 1) * UNIT]
                         .rearrange("p a n -> p (a n)"))
            for tt in range(TT):
                sp.wait_ge(fin, tt + 1)
                sp.dma_start(out[tt * P:(tt + 1) * P, :], ACC[:, tt, :]).then_inc(stored, 16)
            sp.wait_ge(stored, 16 * TT)

        @block.gpsimd
        def _(pool):
            nc.gpsimd.memset(IDENT[:], 0.0).then_inc(consts, 1)
            nc.gpsimd.iota(IOTA[:], [[1, NKEYS]], base=0, channel_multiplier=0,
                           allow_small_or_imprecise_dtypes=True).then_inc(consts, 1)
            pool.wait_ge(consts, 2)
            nc.gpsimd.affine_select(out=IDENT[:], in_=IDENT[:], compare_op=ALU.not_equal, fill=1.0, base=0,
                                    pattern=[[-1, P]], channel_multiplier=1).then_inc(consts, 1)
            loads = [
                (GT[:], gain_t), (BS[:], bs_t), (WST[:], ws_t),
                (ZG[:], z_gain.broadcast_to([P, HALF])), (OG[:], out_gain.broadcast_to([P, HALF])),
                (SG[:], subln_gain.broadcast_to([P, VD])),
                (LAMV[:].rearrange("p a b -> p (a b)"), lambdas.broadcast_to([P, 4 * QK])),
                (ROPE[:], rope),
            ]
            for dst, src in loads:
                pool.dma_start(dst, src).then_inc(small_ready, 16)
            pool.wait_ge(small_ready, 16 * len(loads))
            pool.wait_ge(consts, 3)
            nc.gpsimd.memset(WST[CHUNK:P, :, 0:CHUNK], 0.0).then_inc(consts, 1)
            pool.wait_ge(consts, 4)
            for n in range(BESIDE0 + 1, BESIDE1, 2):
                pool.wait_ge(hi_ready, n + 1)
                pool.wait_ge(used, n - (LO_SLOTS - 1))
                nc.gpsimd.tensor_tensor(LO[:, n % 2, :], RAW[:, n % 4, :], HI[:, n % 4, :].bitcast(FP32),
                                        ALU.subtract).then_inc(lo_ready[n % 2], 1)
            pool.wait_ge(tr_lo, 24)
            pool.dma_start(KEYS[:], keys_t).then_inc(keys_ready, 16)
            pool.wait_ge(x1_ready, 8)
            for tt in range(TT):
                pool.dma_start(x1_dram[tt * P:(tt + 1) * P, :], X[:, tt, :]).then_inc(x1_saved, 16)
            pool.wait_ge(x1_saved, 16 * TT)
            def weigh(rows, tokens, batch):
                pool.wait_ge(one2, batch)
                width = rows.shape[-1]
                nc.gpsimd.tensor_tensor(rows, rows, EG[:, 2, tokens].unsqueeze(2).broadcast_to([P, TOK8, width]),
                                        ALU.mult).then_inc(one2g, 1)

            with pool.Fori(0, N_B) as b:
                weigh(ONES[0][1][:], bass.ds(b * TOK8, TOK8), b + 1)
            pool.wait_ge(used, V0)
            for tt in range(TT):
                pool.dma_start(ACC[:, tt, :], x1_dram[tt * P:(tt + 1) * P, :]).then_inc(x1_back, 16)
            for b in range(N_B, B_ALL):
                weigh(ONES[1][1][:, b % 2], slice(b * TOK8, (b + 1) * TOK8), b + 1)
            with pool.Fori(0, N_B) as b:
                weigh(ONES[2][1][:], bass.ds(b * TOK8, TOK8), b + (B_ALL + 1))
            pool.wait_ge(g_read, B_ALL + N_B)
            pool.wait_ge(used, V0 + 16 * 9)
            pool.dma_start(FG[:], final_gain.broadcast_to([P, D])).then_inc(fg_ready, 16)

        @block.scalar
        def _(act):
            def hi_part(slot):
                nc.scalar.activation(HI[:, slot, :], RAW[:, slot, :], ACT.Copy).then_inc(hi_ready, 1)

            def hi(n):
                act.wait_ge(raw_ready[n % 4], 16 * (n // RAW_SLOTS + 1))
                if n >= HI_SLOTS:
                    act.wait_ge(used, n - (HI_SLOTS - 1))
                hi_part(n % 4)

            def hi_at(it, per, u):
                act.wait_ge(raw_ready[u % 4], it * (4 * per) + 16 * (u // 4 + 1))
                act.wait_ge(used, it * per + (u - (HI_SLOTS - 1)))
                hi_part(u % 4)

            n_sums = [0]

            def squares(src, col, junk):
                if n_sums[0]:
                    act.wait_ge(sums, n_sums[0])
                n_sums[0] += 1
                nc.scalar.activation(junk, src, ACT.Square, accum_out=SS[:, col:col + 1]).then_inc(sums, 1)

            def root(count, dst):
                act.wait_ge(means, count)
                nc.scalar.activation(dst, dst, ACT.Sqrt).then_inc(roots, 1)

            def transposed_hi(kp, bank, count, gain):
                act.wait_ge(tr_done, count)
                for k in (2 * kp, 2 * kp + 1):
                    src = PS[:, bank, (k % 2) * T:(k % 2 + 1) * T]
                    if gain is None:
                        ins = nc.scalar.activation(xT[:, k, 0, :], src, ACT.Copy)
                    else:
                        ins = nc.scalar.activation(xT[:, k, 0, :], src, ACT.Copy, scale=GT[:, gain, k:k + 1])
                ins.then_inc(tr_hi, 1)

            act.dma_start(X[:, 0, :], x[0:P, :]).then_inc(x_ready[0], 16)
            act.dma_start(X[:, 1, :], x[P:T, :]).then_inc(x_ready[1], 16)
            act.wait_ge(x_ready[0], 16)
            nc.scalar.activation(SQX[:, 0, :], X[:, 0, :], ACT.Square, accum_out=SS[:, 4:5]).then_inc(sums0, 1)
            root(1, SS[:, 6:7])
            root(2, SS[:, 7:8])
            for n in range(2):
                hi(n)
            act.wait_ge(small_ready, 16 * 8)
            for kp in range(KT // 2):
                transposed_hi(kp, kp, kp + 1, 0)
                if kp in (1, 3):
                    hi(2 + kp // 2)

            def copy_out(g):
                for tt in range(TT):
                    for c in range(2):
                        act.wait_ge(used, KT * (g + 1))
                        nc.scalar.activation(GRP[:, g, tt, c * BANK:(c + 1) * BANK], PS[:, BANK0[g] + 2 * tt + c, :],
                                             ACT.Gelu_apprx_tanh if g in (Z_, U_) else ACT.Copy).then_inc(evac, 1)

            def heads_out(b):
                act.wait_ge(qk_tr, b + 1)
                nc.scalar.activation((QT, KTr)[b // 4][:, 2 * (b % 4):2 * (b % 4) + 2, :],
                                     PS[:, 4 + b % 4, :].rearrange("p (a b) -> p a b", a=2), ACT.Copy).then_inc(qk_out, 1)

            def exps(c):
                keys = P * (c // HEADS + 1)
                act.wait_ge(maxed, c + 1)
                if c >= 2:
                    act.wait_ge(mixed_probs, c - 1)
                for m in range(2):
                    ins = nc.scalar.activation(PR[:, c % 2, m, 0:keys], PS[:, m, 0:keys], ACT.Exp,
                                               bias=NB[:, c % 2, m:m + 1], scale=QK ** -0.5,
                                               accum_out=LS[:, c % 2, m:m + 1])
                ins.then_inc(exped, 1)

            def probs_out(c):
                tt = c // HEADS
                act.wait_ge(at_done, c + 1)
                if c:
                    act.wait_ge(pv_done, c)
                nc.scalar.activation(AT[:, 0:tt + 1, :], PS[:, 2, 0:P * (tt + 1)].rearrange("p (a b) -> p a b", b=P),
                                     ACT.Copy).then_inc(at_out, 1)

            def head_out(c):
                tt, h = divmod(c, HEADS)
                act.wait_ge(pv_done, c + 1)
                nc.scalar.activation(MIX[:, tt, h * VD:(h + 1) * VD], PS[:, 3, 0:VD], ACT.Copy).then_inc(pv_out, 1)

            for n in range(4, ATT0 + 4):
                hi(n)
                if n % KT == 3 and n > KT:
                    copy_out(n // KT - 1)
                if n >= V_ * KT + 12:
                    heads_out(n - V_ * KT - 12)
            act.wait_ge(lam_sums, 1)
            nc.scalar.activation(LAM[:, 2:4], LAM[:, 0:2], ACT.Exp).then_inc(lam_exp, 1)
            for c in range(COMBOS + 1):
                n = ATT0 + 2 * c + 4
                if c >= 1:
                    probs_out(c - 1)
                if c < COMBOS:
                    exps(c)
                if n < OUT0 + 4:
                    hi(n)
                if c >= 1:
                    head_out(c - 1)
                if n < OUT0 + 4:
                    hi(n + 1)
                if n == ATT0 + KT + 2:
                    copy_out(Z_)
                if n == OUT0 - 2:
                    root(3, GS[:, 0, 1])
                    root(4, GS[:, 1, 1, 0, :])
            copy_out(U_)
            root(5, GS[:, 1, 1, 1, :])
            for kp in range(4):
                transposed_hi(kp, 4 + kp, 8 + kp + 1, None)
            act.wait_ge(sz_read, 16)
            for tt in range(TT):
                squares(MIX[:, tt, HALF:D], tt, JUNK[:])
            root(6, SS[:, 6:8])
            for n in range(OUT0 + 4, OUT0 + 8):
                hi(n)
            for kp in range(4, 8):
                transposed_hi(kp, kp, 8 + kp + 1, None)
            for n in range(OUT0 + 8, WQ0 + 4):
                hi(n)
                if n in (OUT0 + KT + 8, OUT0 + KT + 10):
                    tt = (n - OUT0 - KT - 8) // 2
                    act.wait_ge(x1_ready, 2 * tt + 2)
                    squares(X[:, tt, 0:HALF], tt, JUNK[:])
            for tt in range(TT):
                act.wait_ge(x1_ready, 4 + 2 * tt + 2)
                squares(X[:, tt, HALF:D], 2 + tt, JUNK[:])
            root(7, SS[:, 6:8])
            for kp in range(KT // 2):
                transposed_hi(kp, kp, 16 + kp + 1, 1)
            for n in range(WQ0 + 4, U0 + 4):
                hi(n)

            def gelu(pair, count):
                act.wait_ge(tile_out, count)
                part = store[:, bass.ds(pair * 2, 2), :]
                nc.scalar.activation(part, part, ACT.Gelu_apprx_tanh).then_inc(gelus, 1)

            def first_scores_out(tt):
                for b in range(4):
                    act.wait_ge(sc_done, 4 * tt + b + 1)
                    nc.scalar.activation(SC[:, tt, 4 * b:4 * b + 4, :],
                                         PS[:, 4 + b, :].rearrange("p (a b) -> p a b", b=NKEYS), ACT.Copy).then_inc(sc_out, 1)

            def picks_to_rows(tt):
                act.wait_ge(picks_tr, tt + 1)
                nc.scalar.activation(EG[:, :, tt * P:(tt + 1) * P],
                                     PS[:, 7 - tt, 0:3 * P].rearrange("p (a b) -> p a b", b=P), ACT.Copy).then_inc(picks_out, 1)

            def pair_hi(i):
                for r in range(4):
                    hi_at(i, 4, U0 + r)

            for i in range(1, SPREAD1):
                pair_hi(i)
                if i == 1:
                    first_scores_out(0)
                    first_scores_out(1)
                if i in GATES_AT:
                    act.wait_ge(best_ready, GATES_AT.index(i) + 1)
                    nc.scalar.activation(ROWS[:, 2, :], ROWS[:, 2, :], ACT.Exp).then_inc(gexp, 1)
                if i in PICKS_AT:
                    picks_to_rows(PICKS_AT.index(i))
                gelu(i - 1, 2 * i + HC)
            with act.Fori(SPREAD1, PAIRS) as i:
                pair_hi(i)
                gelu(i - 1, i * 2 + HC)
            gelu(PAIRS - 1, HC + NKEYS)

            def weight_hi(g, s):
                act.wait_ge(used, g * 16 + (V0 - 16 + 9 + s))
                nc.scalar.activation(WHL[:, s, 0, :], store[:, bass.ds(g * VG + s, 1), :].rearrange("p a t -> p (a t)"),
                                     ACT.Copy).then_inc(w_hi, 1)

            for u in range(4):
                hi(V0 + u)
            act.wait_ge(g_read, B_ALL)
            for s in range(4):
                weight_hi(0, s)

            def values(g, first=False, last=False, spread=False):
                for u in range(16):
                    if not (first and u < 4):
                        hi_at(g, 16, V0 + u)
                    if u < 4:
                        weight_hi(g, u + 4)
                    if u >= 12 and not last:
                        if spread and u == 12:
                            act.wait_ge(g_read, g * B2 + B_ALL)
                        weight_hi(g + 1, u - 12)

            values(0, first=True)
            with act.Fori(1, E2A // VG) as g:
                values(g, spread=True)
            with act.Fori(E2A // VG, N_VG - 1) as g:
                values(g)
            values(N_VG - 1, last=True)
            act.wait_ge(flushed, 8 * N_VG - 4)
            act.wait_ge(fg_ready, 16)
            for tt in range(TT):
                squares(ACC[:, tt, 0:HALF], tt, FJ[:])
            for tt in range(TT):
                act.wait_ge(flushed, 8 * N_VG - 2 + 2 * tt)
                squares(ACC[:, tt, HALF:D], 2 + tt, FJ[:])
            root(8, SS[:, 6:8])
            act.wait_ge(scaled, 1)
            nc.scalar.activation(ACC[:, 1, :], ACC[:, 1, :], ACT.Copy, scale=SS[:, 9:10]).then_inc(act_scaled, 1)

        @block.vector
        def _(dve):
            chain = [0]
            v = nc.vector

            def link(ins):
                chain[0] += 1
                ins.then_inc(dve_chain, 1)
                dve.wait_ge(dve_chain, chain[0])

            def split(u):
                v.tensor_tensor(LO[:, u % 2, :], RAW[:, u % 4, :], HI[:, u % 4, :].bitcast(FP32),
                                ALU.subtract).then_inc(lo_ready[u % 2], 1)

            def lo(n):
                if BESIDE0 <= n < BESIDE1 and n % 2:
                    return
                dve.wait_ge(hi_ready, n + 1)
                if n >= LO_SLOTS:
                    dve.wait_ge(used, n - (LO_SLOTS - 1))
                split(n)

            def lo_at(it, per, u):
                dve.wait_ge(hi_ready, it * per + (u + 1))
                dve.wait_ge(used, it * per + (u - (LO_SLOTS - 1)))
                split(u)

            def mean(dst, src, n):
                v.tensor_scalar(dst, src, 1.0 / n, EPS, ALU.mult, ALU.add).then_inc(means, 1)

            def transposed_lo(kp, bank, count, gain):
                dve.wait_ge(tr_hi, count)
                for k in (2 * kp, 2 * kp + 1):
                    src = PS[:, bank, (k % 2) * T:(k % 2 + 1) * T]
                    hi_part = xT[:, k, 0, :].bitcast(FP32)
                    if gain is None:
                        ins = v.tensor_tensor(xT[:, k, 1, :], src, hi_part, ALU.subtract)
                    else:
                        ins = v.scalar_tensor_tensor(xT[:, k, 1, :], src, GT[:, gain, k:k + 1], hi_part,
                                                     ALU.mult, ALU.subtract)
                ins.then_inc(tr_lo, 1)

            def scale_rows(tt):
                v.tensor_scalar(XS[:, tt, :], X[:, tt, :], SS[:, 8 + tt:9 + tt], None, ALU.mult).then_inc(rows_ready, 1)

            dve.wait_ge(x_ready[1], 16)
            link(v.tensor_tensor(SQX[:, 1, :], X[:, 1, :], X[:, 1, :], ALU.mult))
            dve.wait_ge(sums0, 1)
            mean(SS[:, 6:7], SS[:, 4:5], D)
            link(v.tensor_reduce(SS[:, 5:6], SQX[:, 1, :], AX.X, ALU.add))
            mean(SS[:, 7:8], SS[:, 5:6], D)
            for tt in range(TT):
                dve.wait_ge(roots, tt + 1)
                link(v.reciprocal(SS[:, 8 + tt:9 + tt], SS[:, 6 + tt:7 + tt]))
                scale_rows(tt)
            for n in range(2):
                lo(n)
            for kp in range(KT // 2):
                transposed_lo(kp, kp, kp + 1, 0)

            def group_sums(rows, which, tt):
                link(v.tensor_tensor(SQ[:], rows, rows, ALU.mult))
                link(v.tensor_reduce(GS[:, which, 0, tt, :], SQ[:].rearrange("p (a b) -> p a b", b=P), AX.X, ALU.add))

            def group_scale(rows, which, tt, gain):
                link(v.reciprocal(GS[:, which, 2, tt, :], GS[:, which, 1, tt, :]))
                by = rows.rearrange("p (a b) -> p a b", b=P)
                link(v.tensor_tensor(by, by, GS[:, which, 2, tt, :].unsqueeze(2).broadcast_to([P, 8, P]), ALU.mult))
                return v.tensor_tensor(by, by, gain, ALU.mult)

            def rotate(g, tt):
                rows = GRP[:, g, tt, :].rearrange("p (b d) -> p b d", d=QK)
                first, second = rows[:, :, 0:ROT], rows[:, :, ROT:2 * ROT]
                cos, sin = (ROPE[:, i, tt, :].unsqueeze(1).broadcast_to([P, 2 * HEADS, ROT]) for i in range(2))
                v.tensor_tensor(RT[:, 0], first, cos, ALU.mult)
                v.tensor_tensor(RT[:, 1], second, sin, ALU.mult)
                v.tensor_tensor(RT[:, 2], second, cos, ALU.mult)
                link(v.tensor_tensor(RT[:, 3], first, sin, ALU.mult))
                v.tensor_tensor(first, RT[:, 0], RT[:, 1], ALU.subtract)
                v.tensor_tensor(second, RT[:, 2], RT[:, 3], ALU.add).then_inc(roped, 1)
                dve.wait_ge(roped, 2 * g + tt + 1)

            def minus_lambda():
                maps = SQ[:, 0:2 * QK].rearrange("p (a b) -> p a b", a=2)
                link(v.tensor_tensor(maps, LAMV[:, 0:4:2, :], LAMV[:, 1:4:2, :], ALU.mult))
                v.tensor_reduce(LAM[:, 0:2], maps, AX.X, ALU.add).then_inc(lam_sums, 1)

            for n in range(2, ATT0 + 2):
                lo(n)
                for g in (Q_, K_):
                    if n in (KT * (g + 1) + 4, KT * (g + 1) + 6):
                        dve.wait_ge(evac, 4 * (g + 1))
                        rotate(g, (n - KT * (g + 1) - 4) // 2)
                if n == ATT0 - 4:
                    minus_lambda()
            dve.wait_ge(lam_exp, 1)
            link(v.tensor_tensor(LAM[:, 4:5], LAM[:, 3:4], LAM[:, 2:3], ALU.subtract))
            link(v.tensor_scalar(LAM[:, 5:6], LAM[:, 4:5], -LAMBDA_INIT, None, ALU.add))

            def masked_max(c):
                tt = c // HEADS
                keys = P * (tt + 1)
                dve.wait_ge(scored, c + 1)
                link(v.memset(PS[0:CHUNK, 0:2, keys - CHUNK:keys], NEG))
                link(v.tensor_reduce(RL[:, c % 2, :], PS[:, 0:2, 0:keys], AX.X, ALU.max))
                v.tensor_scalar(NB[:, c % 2, :], RL[:, c % 2, :], -(QK ** -0.5), None, ALU.mult).then_inc(maxed, 1)

            def subtract_maps(c):
                keys = P * (c // HEADS + 1)
                dve.wait_ge(exped, c + 1)
                if c >= 2:
                    dve.wait_ge(at_done, c - 1)
                link(v.reciprocal(RL[:, c % 2, :], LS[:, c % 2, :]))
                link(v.tensor_tensor(RL[:, c % 2, 1:2], RL[:, c % 2, 1:2], LAM[:, 5:6], ALU.mult))
                link(v.tensor_scalar(PR[:, c % 2, 1, 0:keys], PR[:, c % 2, 1, 0:keys], RL[:, c % 2, 1:2], None, ALU.mult))
                v.scalar_tensor_tensor(AM[:, c % 2, 0:keys], PR[:, c % 2, 0, 0:keys], RL[:, c % 2, 0:1],
                                       PR[:, c % 2, 1, 0:keys], ALU.mult, ALU.add).then_inc(mixed_probs, 1)

            z_gain3 = ZG[:].rearrange("p (a b) -> p a b", b=P)
            s_gain3 = SG[:].unsqueeze(1).broadcast_to([P, HEADS, VD])
            heads_of = [MIX[:, tt, 0:HALF] for tt in range(TT)]
            z_of = [GRP[:, Z_, tt, :] for tt in range(TT)]
            link(v.tensor_scalar(SG[:], SG[:], 1.0 - LAMBDA_INIT, None, ALU.mult))
            for c in range(COMBOS):
                lo(ATT0 + 2 * c + 2)
                masked_max(c)
                lo(ATT0 + 2 * c + 3)
                if c == 10:
                    dve.wait_ge(evac, 16)
                if c in (10, 11):
                    group_sums(z_of[c - 10], 0, c - 10)
                if c == 11:
                    mean(GS[:, 0, 1], GS[:, 0, 0], P)
                if c == 12:
                    dve.wait_ge(pv_out, HEADS)
                    group_sums(heads_of[0], 1, 0)
                    mean(GS[:, 1, 1, 0, :], GS[:, 1, 0, 0, :], P)
                subtract_maps(c)
            dve.wait_ge(roots, 4)
            for tt in range(TT):
                group_scale(z_of[tt], 0, tt, z_gain3).then_inc(z_ready, 1)
            group_scale(heads_of[0], 1, 0, s_gain3)
            dve.wait_ge(pv_out, COMBOS)
            group_sums(heads_of[1], 1, 1)
            mean(GS[:, 1, 1, 1, :], GS[:, 1, 0, 1, :], P)
            dve.wait_ge(roots, 5)
            group_scale(heads_of[1], 1, 1, s_gain3).then_inc(heads_ready, 1)
            for tt in range(TT):
                for g in range(GROUPS):
                    dve.wait_ge(sz_done, 2 * tt + g // 4 + 1)
                    v.scalar_tensor_tensor(MIX[:, tt, HALF + g * P:HALF + (g + 1) * P],
                                           PS[:, 2 * tt + g // 4, (g % 4) * P:(g % 4 + 1) * P],
                                           BS[:, g:g + 1], GRP[:, U_, tt, g * P:(g + 1) * P],
                                           ALU.add, ALU.mult).then_inc(sz_read, 1)
            for kp in range(4):
                transposed_lo(kp, 4 + kp, 8 + kp + 1, None)
            lo(OUT0 + 2)
            dve.wait_ge(sums, 2)
            mean(SS[:, 6:8], SS[:, 0:2], HALF)
            lo(OUT0 + 3)
            dve.wait_ge(roots, 6)
            link(v.reciprocal(SS[:, 8:10], SS[:, 6:8]))
            for tt in range(TT):
                v.scalar_tensor_tensor(MIX[:, tt, HALF:D], MIX[:, tt, HALF:D], SS[:, 8 + tt:9 + tt], OG[:],
                                       ALU.mult, ALU.mult).then_inc(rows_ready, 1)
                lo(OUT0 + 4 + tt)
            for kp in range(4, 8):
                transposed_lo(kp, kp, 8 + kp + 1, None)
                if kp % 2:
                    lo(OUT0 + 6 + kp // 2 - 2)
            def residual(g, b):
                tt, c = divmod(b, 2)
                cols = slice(g * UNIT + c * BANK, g * UNIT + (c + 1) * BANK)
                v.tensor_tensor(X[:, tt, cols], PS[:, 4 * g + b, :], X[:, tt, cols], ALU.add).then_inc(x1_ready, 1)

            for n in range(OUT0 + 8, WQ0 + 2):
                lo(n)
                if OUT0 + KT + 2 <= n < OUT0 + KT + 6:
                    residual(0, n - OUT0 - KT - 2)
            for b in range(4):
                residual(1, b)
            dve.wait_ge(sums, 6)
            link(v.tensor_tensor(SS[:, 4:6], SS[:, 0:2], SS[:, 2:4], ALU.add))
            mean(SS[:, 6:8], SS[:, 4:6], D)
            dve.wait_ge(roots, 7)
            link(v.reciprocal(SS[:, 8:10], SS[:, 6:8]))
            for tt in range(TT):
                scale_rows(tt)
            for kp in range(KT // 2):
                transposed_lo(kp, kp, 16 + kp + 1, 1)

            def add_halves(dst, bank):
                v.tensor_reduce(dst, PS[:, bank, :].rearrange("p (a t) -> p t a", a=2), AX.X, ALU.add).then_inc(tile_out, 1)

            def query(c):
                dve.wait_ge(used, WQ0 + 2 * c + 2)
                add_halves(QTQ[:, c, :], c % 2)

            for n in range(WQ0 + 2, U0 + 2):
                lo(n)
                if n % 2 and n >= WQ0 + 3:
                    query((n - WQ0 - 3) // 2)

            grid = [P, PH // 2, TOPK, TOPK]

            def top16(row, values, places):
                link(v.max(values[:, 0:8], row))
                v.max_index(places[:, 0:8], values[:, 0:8], row)
                link(v.match_replace(row, values[:, 0:8], row, FLOOR))
                link(v.max(values[:, 8:16], row))
                link(v.max_index(places[:, 8:16], values[:, 8:16], row))

            def choice(tt):
                for c in range(HC):
                    dve.wait_ge(sc_out, 4 * tt + c // 4 + 1)
                    top16(SC[:, tt, c, :], S16[:, tt, c, :], I16[:, tt, c, :])
                    yield
                link(v.tensor_copy(I16F[:, tt], I16[:, tt]))
                s1, s2 = S16[:, tt, 0:HC:2, :], S16[:, tt, 1:HC:2, :]
                lists = I16F[:, tt, 0:HC:2, :], I16F[:, tt, 1:HC:2, :]
                heads = [slice(0, PH // 2), slice(PH // 2, PH)]
                for hs in heads:
                    link(v.tensor_tensor(CAND[:, hs], s1[:, hs].unsqueeze(3).broadcast_to(grid),
                                         s2[:, hs].unsqueeze(2).broadcast_to(grid), ALU.add))
                    yield
                for h in range(PH):
                    top16(CAND[:, h].rearrange("p a b -> p (a b)"), BEST[:, h], CI[:, h])
                    yield
                if tt:
                    dve.wait_ge(picks_tr, 1)
                gates = ROWS[:, 2].rearrange("p (h k) -> p h k", h=PH)
                v.tensor_tensor(gates, BEST[:], BEST[:, :, 0:1].broadcast_to([P, PH, TOPK]), ALU.subtract)\
                    .then_inc(best_ready, 1)
                for half, (op, by) in enumerate(((ALU.logical_shift_right, 4), (ALU.bitwise_and, 15))):
                    link(v.tensor_scalar(CIA[:], CI[:], by, None, op))
                    link(v.tensor_copy(CF[:], CIA[:]))
                    yield
                    for hs in heads:
                        link(v.tensor_tensor(EQ[:, hs], CF[:, hs].unsqueeze(3).broadcast_to(grid),
                                             IOTA[:, 0:TOPK].unsqueeze(1).unsqueeze(1).broadcast_to(grid), ALU.is_equal))
                        yield
                        link(v.tensor_tensor(EQ[:, hs], EQ[:, hs], lists[half][:, hs].unsqueeze(2).broadcast_to(grid), ALU.mult))
                        yield
                        link(v.tensor_reduce(ROWS[:, half].rearrange("p (h k) -> p h k", h=PH)[:, hs], EQ[:, hs], AX.X, ALU.add))
                        yield
                dve.wait_ge(gexp, tt + 1)
                link(v.tensor_reduce(GM[:, 0, :], gates, AX.X, ALU.add))
                link(v.reciprocal(GM[:, 1, :], GM[:, 0, :]))
                v.tensor_tensor(gates, gates, GM[:, 1, :].unsqueeze(2).broadcast_to([P, PH, TOPK]), ALU.mult).then_inc(picks, 1)
                yield

            def score(j, bank, units):
                dve.wait_ge(used, units)
                add_halves(store[:, bass.ds(j, 1), :].rearrange("p a t -> p (a t)"), bank)

            for n in (U0 + 2, U0 + 3):
                lo(n)
            dve.wait_ge(x1_saved, 16 * TT)
            score(0, 0, U0 + 2)

            pieces = choice(0), choice(1)
            done = [0, 0]

            def piece(i):
                tt = 0 if done[0] < PIECES else 1
                if done[tt] < PIECES:
                    next(pieces[tt])
                    done[tt] += 1

            for i in range(1, SPREAD1):
                for r in range(4):
                    lo_at(i, 4, U0 + r)
                    if r == 1:
                        score(2 * i - 1, 1, 4 * i + U0)
                    if r == 3:
                        score(2 * i, 0, 4 * i + U0 + 2)
                    if i >= 2:
                        piece(i)
            assert done == [PIECES, PIECES]
            dve.wait_ge(picks_out, TT)

            def one_hot(dst, row, tokens, j0, signal):
                width = dst.shape[-1]
                v.tensor_tensor(dst, IOTA[:, j0:j0 + width].unsqueeze(1).broadcast_to([P, TOK8, width]),
                                EG[:, row, tokens].unsqueeze(2).broadcast_to([P, TOK8, width]),
                                ALU.is_equal).then_inc(signal, 1)

            def rows_of(which, b, j0, count):
                dve.wait_ge(g_done, count)
                one_hot(ONES[which][0][:], 0, bass.ds(b * TOK8, TOK8), 0, one1)
                one_hot(ONES[which][1][:], 1, bass.ds(b * TOK8, TOK8), j0, one2)

            def apply_gates(b, bank, j0, count):
                dve.wait_ge(g_done, count)
                part = store[:, j0:j0 + E2A, bass.ds(b * TOK8, TOK8)]
                v.tensor_tensor(part, part, PS[:, bank, :].rearrange("p (t j) -> p j t", t=TOK8), ALU.mult).then_inc(g_read, 1)

            def pair(i, before=None, after=None):
                for r in range(4):
                    lo_at(i, 4, U0 + r)
                    if r == 0 and before:
                        before()
                    if r == 1:
                        score(i * 2 - 1, 1, i * 4 + U0)
                    if r == 2 and after:
                        after()
                    if r == 3:
                        score(i * 2, 0, i * 4 + (U0 + 2))

            def first_rows():
                one_hot(ONES[0][0][:], 0, slice(0, TOK8), 0, one1)
                one_hot(ONES[0][1][:], 1, slice(0, TOK8), 0, one2)

            pair(SPREAD1, after=first_rows)
            dve.wait_ge(gelus, SPREAD1)
            with dve.Fori(SPREAD1 + 1, SPREAD1 + N_B) as i:
                pair(i, before=lambda: apply_gates(i - (SPREAD1 + 1), 2, 0, i - SPREAD1),
                     after=lambda: rows_of(0, i - SPREAD1, 0, i - SPREAD1))
            pair(SPREAD1 + N_B, before=lambda: apply_gates(N_B - 1, 2, 0, N_B))
            with dve.Fori(SPREAD1 + N_B + 1, PAIRS) as i:
                pair(i)
            score(NKEYS - 1, 1, V0)
            for u in range(2):
                lo(V0 + u)

            def all_rows(b):
                if b >= N_B + 2:
                    dve.wait_ge(g_done, b - 1)
                for row, signal in ((0, one1), (1, one2)):
                    one_hot(ONES[1][row][:, b % 2], row, slice(b * TOK8, (b + 1) * TOK8), 0, signal)

            dve.wait_ge(g_done, N_B)
            all_rows(N_B)
            all_rows(N_B + 1)
            dve.wait_ge(gelus, PAIRS)
            for b in range(N_B, B_ALL):
                dve.wait_ge(g_done, b + 1)
                part = store[:, :, b * TOK8:(b + 1) * TOK8]
                v.tensor_tensor(part, part, PS[:, 2 * (b - N_B):2 * (b - N_B) + 2, :].rearrange("p a (t j) -> p j (a t)", t=4),
                                ALU.mult).then_inc(g_read, 1)
                if b + 2 < B_ALL:
                    all_rows(b + 2)
            dve.wait_ge(g_read, B_ALL)

            def weight_lo(g, s):
                dve.wait_ge(w_hi, g * VG + (s + 1))
                v.tensor_tensor(WHL[:, s, 1, :], store[:, bass.ds(g * VG + s, 1), :].rearrange("p a t -> p (a t)"),
                                WHL[:, s, 0, :].bitcast(FP32), ALU.subtract).then_inc(w_lo, 1)

            def flush(g, h, b, onto_first):
                dve.wait_ge(used, g * 16 + (V0 + 8 * h + 8))
                tt, c = divmod(b, 2)
                cols = slice(h * UNIT + c * BANK, h * UNIT + (c + 1) * BANK)
                if not onto_first:
                    dve.wait_ge(flushed, g * 8 + (4 * h + b - 7))
                v.tensor_tensor(ACC[:, tt, cols], PS[:, 4 * h + b, :], ACC[:, tt, cols], ALU.add).then_inc(flushed, 1)

            def values(g, first=False, second=False, last=False, spread=False):
                for u in range(16):
                    if not (first and u < 2):
                        lo_at(g, 16, V0 + u)
                    if u < 4:
                        weight_lo(g, u + 4)
                    if u >= 12 and not last:
                        if spread and u == 12:
                            apply_gates(g * B2 + (3 - B2), 0, E2A, g * B2 + B_ALL)
                        weight_lo(g + 1, u - 12)
                    if 1 <= u <= 4 and not first:
                        flush(g - 1, 1, u - 1, second)
                    if 9 <= u <= 12:
                        flush(g, 0, u - 9, first)
                    if spread and u in SPREAD_U:
                        s = SPREAD_U.index(u)
                        rows_of(2, g * B2 + (s - B2), E2A, g * B2 + (B_ALL - B2 + s))
                    if spread and u - 2 in SPREAD_U[:3]:
                        s = SPREAD_U.index(u - 2)
                        apply_gates(g * B2 + (s - B2), 4 + s, E2A, g * B2 + (B_ALL - B2 + s + 1))

            for s in range(4):
                weight_lo(0, s)
            dve.wait_ge(x1_back, 16 * TT)
            values(0, first=True)
            values(1, second=True, spread=True)
            with dve.Fori(2, E2A // VG) as g:
                values(g, spread=True)
            with dve.Fori(E2A // VG, N_VG - 1) as g:
                values(g)
            values(N_VG - 1, last=True)
            for b in range(4):
                flush(N_VG - 1, 1, b, False)
            dve.wait_ge(sums, 10)
            link(v.tensor_tensor(SS[:, 4:6], SS[:, 0:2], SS[:, 2:4], ALU.add))
            mean(SS[:, 6:8], SS[:, 4:6], D)
            dve.wait_ge(roots, 8)
            v.reciprocal(SS[:, 8:10], SS[:, 6:8]).then_inc(scaled, 1)
            dve.wait_ge(scaled, 1)
            v.scalar_tensor_tensor(ACC[:, 0, :], ACC[:, 0, :], SS[:, 8:9], FG[:], ALU.mult, ALU.mult).then_inc(fin, 1)
            dve.wait_ge(act_scaled, 1)
            v.tensor_tensor(ACC[:, 1, :], ACC[:, 1, :], FG[:], ALU.mult).then_inc(fin, 1)

        @block.tensor
        def _(pe):
            mm = nc.tensor.matmul

            def transpose_tiles(src, tiles, bank, tt):
                for k in tiles:
                    b = bank + (k - tiles[0]) // 2
                    last = nc.tensor.transpose(PS[:, b, (k % 2) * T + tt * P:(k % 2) * T + (tt + 1) * P],
                                               src[:, tt, k * P:(k + 1) * P], IDENT[:])
                    if tt == TT - 1 and k % 2:
                        last.then_inc(tr_done, 1)

            def row_unit(u, bank, high, low, first, last, free=None):
                h, l = HI[:, u % 4, :], LO[:, u % 2, :]
                for tt in range(TT):
                    if free:
                        free(tt)
                    for c in range(2):
                        cols = slice(c * BANK, (c + 1) * BANK)
                        mm(PS[:, bank + 2 * tt + c, :], high(tt), h[:, cols], start=first, stop=False)
                        mm(PS[:, bank + 2 * tt + c, :], high(tt), l[:, cols], start=False, stop=False)
                    for c in range(2):
                        cols = slice(c * BANK, (c + 1) * BANK)
                        ins = mm(PS[:, bank + 2 * tt + c, :], low(tt), h[:, cols], start=False, stop=last)
                ins.then_inc(used, 1)

            def column_unit(u, bank, ready=None):
                for kk in range(KT // 2):
                    k = (KT // 2) * (u % 2) + kk
                    cols = slice(kk * P, (kk + 1) * P)
                    if ready:
                        ready(k)
                    if kk:
                        mm(PS[:, bank, 0:T], LO[:, u % 2, cols], xT[:, k, 0, :], start=False, stop=False)
                    ins = mm(PS[:, bank, :], HI[:, u % 4, cols], xT[:, k].rearrange("p a t -> p (a t)"),
                             start=k == 0, stop=k == KT - 1)
                    if not kk:
                        ins = mm(PS[:, bank, 0:T], LO[:, u % 2, cols], xT[:, k, 0, :], start=False, stop=False)
                ins.then_inc(used, 1)

            def x_part(k, part):
                return lambda tt: xT[:, k, part, tt * P:(tt + 1) * P]

            def lo_wait(n):
                pe.wait_ge(lo_ready[n % 2], n // 2 + 1)

            pe.wait_ge(consts, 3)
            for tt in range(TT):
                pe.wait_ge(rows_ready, tt + 1)
                transpose_tiles(XS, range(KT), 0, tt)

            def heads_transposed(b):
                g = (Q_, K_)[b // 4]
                pe.wait_ge(roped, 2 * g + 2)
                if b >= 4:
                    pe.wait_ge(qk_out, b - 3)
                for h in (2 * (b % 4), 2 * (b % 4) + 1):
                    for tt in range(TT):
                        last = nc.tensor.transpose(PS[:, 4 + b % 4, (h % 2) * T + tt * P:(h % 2) * T + (tt + 1) * P],
                                                   GRP[:, g, tt, h * P:(h + 1) * P], IDENT[:])
                last.then_inc(qk_tr, 1)

            def scores(c):
                tt, h = divmod(c, HEADS)
                keys = P * (tt + 1)
                if c:
                    pe.wait_ge(exped, c)
                for m in range(2):
                    half = slice(QK * m, QK * (m + 1))
                    last = mm(PS[:, m, 0:keys], QT[half, h, tt * P:(tt + 1) * P], KTr[half, h, 0:keys],
                              start=True, stop=True)
                last.then_inc(scored, 1)

            def probs_transposed(c):
                pe.wait_ge(mixed_probs, c + 1)
                if c:
                    pe.wait_ge(at_out, c)
                for kt in range(c // HEADS + 1):
                    last = nc.tensor.transpose(PS[:, 2, kt * P:(kt + 1) * P], AM[:, c % 2, kt * P:(kt + 1) * P], IDENT[:])
                last.then_inc(at_done, 1)

            def times_values(c):
                tt, h = divmod(c, HEADS)
                pe.wait_ge(at_out, c + 1)
                if c:
                    pe.wait_ge(pv_out, c)
                for kt in range(tt + 1):
                    last = mm(PS[:, 3, 0:VD], AT[:, kt, :], GRP[:, V_, kt, h * VD:(h + 1) * VD],
                              start=kt == 0, stop=kt == tt)
                last.then_inc(pv_done, 1)

            for g in range(5):
                for k in range(KT):
                    n = g * KT + k
                    free = None
                    if g == 0:
                        pe.wait_ge(tr_lo, max(4, k // 2 + 1))
                    if g == 1 and k == 0:
                        pe.wait_ge(tr_lo, 8)
                    if k == 0 and g in (V_, U_):
                        pe.wait_ge(evac, 4 * (g - 1))
                        if g == U_:
                            def free(tt):
                                pe.wait_ge(evac, 4 * Z_ + 2 * tt + 2)
                    if k == 0 and g == Z_:
                        pe.wait_ge(qk_out, 8)
                    lo_wait(n)
                    row_unit(n, BANK0[g], x_part(k, 0), x_part(k, 1), k == 0, k == KT - 1, free)
                    if g == V_ and k >= 8:
                        heads_transposed(k - 8)
                    if g in (Z_, U_):
                        c = (n - ATT0) // 2
                        if k % 2 == 0:
                            if c == 0:
                                pe.wait_ge(evac, 12)
                            scores(c)
                            if c:
                                probs_transposed(c - 1)
                        elif c:
                            times_values(c - 1)
            probs_transposed(COMBOS - 1)
            times_values(COMBOS - 1)
            pe.wait_ge(consts, 4)
            pe.wait_ge(pv_out, COMBOS)
            for tt in range(TT):
                pe.wait_ge(z_ready, tt + 1)
                for g in range(GROUPS):
                    last = mm(PS[:, 2 * tt + g // 4, (g % 4) * P:(g % 4 + 1) * P], WST[:, g, :],
                              GRP[:, Z_, tt, g * P:(g + 1) * P], start=True, stop=True)
                    if g % 4 == 3:
                        last.then_inc(sz_done, 1)
            pe.wait_ge(evac, 20)
            pe.wait_ge(heads_ready, 1)
            for tt in range(TT):
                transpose_tiles(MIX, range(8), 4, tt)
            pe.wait_ge(sz_read, 16)
            for g in range(2):
                for k in range(KT):
                    n = OUT0 + g * KT + k
                    if g == 0:
                        pe.wait_ge(tr_lo, 8 + k // 2 + 1)
                        if k == 5:
                            pe.wait_ge(rows_ready, 4)
                            pe.wait_ge(tr_lo, 12)
                            for tt in range(TT):
                                transpose_tiles(MIX, range(8, 16), 4, tt)
                    elif k == 0:
                        pe.wait_ge(tr_lo, 16)
                    lo_wait(n)
                    row_unit(n, 4 * g, x_part(k, 0), x_part(k, 1), k == 0, k == KT - 1)
            pe.wait_ge(x1_ready, 8)
            for tt in range(TT):
                pe.wait_ge(rows_ready, 4 + tt + 1)
                transpose_tiles(XS, range(KT), 0, tt)
            for u in range(N_WQ):
                lo_wait(WQ0 + u)
                if u % 2 == 0 and u >= 4:
                    pe.wait_ge(tile_out, u // 2 - 1)
                column_unit(u, (u // 2) % 2, (lambda k: pe.wait_ge(tr_lo, 16 + max(2, k // 2 + 1))) if u < 2 else None)

            def pair(i):
                for r in range(4):
                    pe.wait_ge(lo_ready[r % 2], i * 2 + ((U0 + r) // 2 + 1))
                    if r % 2 == 0:
                        pe.wait_ge(tile_out, i * 2 + (HC + r // 2 - 1))
                    column_unit(r, r // 2)

            def picks_transposed(tt):
                pe.wait_ge(picks, tt + 1)
                for r in range(3):
                    last = nc.tensor.transpose(PS[:, 7 - tt, r * P:(r + 1) * P], ROWS[:, r, :], IDENT[:])
                last.then_inc(picks_tr, 1)

            pair(0)
            pe.wait_ge(tile_out, HC)
            pe.wait_ge(keys_ready, 16)
            for tt in range(TT):
                for b in range(4):
                    if tt:
                        pe.wait_ge(sc_out, b + 1)
                    for c in range(4 * b, 4 * b + 4):
                        last = mm(PS[:, 4 + b, (c % 4) * NKEYS:(c % 4 + 1) * NKEYS], QTQ[:, c, tt * P:(tt + 1) * P],
                                  KEYS[:, c, :], start=True, stop=True)
                    last.then_inc(sc_done, 1)
            with pe.Fori(1, PICKS_AT[0]) as i:
                pair(i)
            pe.wait_ge(sc_out, 8)
            picks_transposed(0)
            with pe.Fori(PICKS_AT[0], PICKS_AT[1]) as i:
                pair(i)
            picks_transposed(1)
            for i in range(PICKS_AT[1], SPREAD1):
                pair(i)

            def spread(rows, bank, count, free):
                pe.wait_ge(one1, count)
                pe.wait_ge(one2g, count)
                if free is not None:
                    pe.wait_ge(g_read, free)
                width = rows[1].shape[-1]
                per = BANK // width
                for t in range(TOK8):
                    last = mm(PS[:, bank + t // per, (t % per) * width:(t % per + 1) * width], rows[0][:, t, :],
                              rows[1][:, t, :], start=True, stop=True)
                last.then_inc(g_done, 1)

            pair(SPREAD1)
            spread([r[:] for r in ONES[0]], 2, 1, None)
            with pe.Fori(SPREAD1 + 1, SPREAD1 + N_B) as i:
                pair(i)
                spread([r[:] for r in ONES[0]], 2, i - (SPREAD1 - 1), i - SPREAD1)
            with pe.Fori(SPREAD1 + N_B, PAIRS) as i:
                pair(i)
            pe.wait_ge(tile_out, HC + NKEYS)
            pe.wait_ge(g_read, N_B)
            for b in range(N_B, B_ALL):
                spread([r[:, b % 2] for r in ONES[1]], 2 * (b - N_B), b + 1, None)

            def values(g, first=False, spreads=False):
                for u in range(16):
                    h, jj = divmod(u, VG)
                    pe.wait_ge(lo_ready[u % 2], g * 8 + ((V0 + u) // 2 + 1))
                    if h == 0:
                        pe.wait_ge(w_lo, g * VG + (jj + 1))
                    if jj == 0 and not first:
                        pe.wait_ge(flushed, g * 8 + (4 * h - 4))
                        if spreads and h:
                            pe.wait_ge(g_read, g * B2 + (B_ALL - 1))
                    if jj == 0 and not first and not h:
                        pe.wait_ge(g_read, (g - 1) * B2 + B_ALL if spreads else B_ALL + N_B)
                    row_unit(u, 4 * h, lambda tt: WHL[:, jj, 0, tt * P:(tt + 1) * P],
                             lambda tt: WHL[:, jj, 1, tt * P:(tt + 1) * P], jj == 0, jj == VG - 1)
                    if spreads and u in SPREAD_U:
                        s = SPREAD_U.index(u)
                        bank = 4 + s if s < 3 else 0
                        pe.wait_ge(flushed, g * 8 + (s - 3 if s < 3 else 1))
                        spread([r[:] for r in ONES[2]], bank, g * B2 + (B_ALL - B2 + s + 1), None)

            pe.wait_ge(g_read, B_ALL)
            values(0, first=True)
            with pe.Fori(1, E2A // VG) as g:
                values(g, spreads=True)
            with pe.Fori(E2A // VG, N_VG) as g:
                values(g)


def kernel(**inputs):
    import concourse.bacc as bacc
    from concourse.bass_utils import run_bass_kernel_spmd

    a = {k: np.asarray(w) for k, w in inputs.items()}
    inv = (500000.0 ** (-np.arange(0, 2 * ROT, 2, dtype=np.float32) / np.float32(2 * ROT))).astype(np.float32)
    ang = np.arange(T, dtype=np.float32)[:, None] * inv[None, :]
    rope = np.stack([np.cos(ang), np.sin(ang)]).astype(np.float32)
    arrays = {
        "x": a["x"].reshape(T, D),
        "w_in": a["w_in"][0],
        "w_out": a["w_out"][0],
        "wq_t": a["peer_w_q"][0].reshape(KT, P, HC, P).transpose(2, 1, 0, 3).reshape(HC, P, D),
        "keys_t": a["peer_sub_keys"][0].transpose(3, 0, 1, 2).reshape(P, HC, NKEYS),
        "u_t": a["peer_u"][0].reshape(NKEYS, NKEYS, KT, P).transpose(1, 3, 2, 0).reshape(NKEYS, P, D),
        "peer_v": a["peer_v"][0],
        "ws_t": a["gmlp_w_s"][0].transpose(2, 0, 1),
        "bs_t": a["gmlp_b_s"][0].T,
        "gain_t": np.stack([a["mix_norm_g"][0].reshape(KT, P), a["ffn_norm_g"][0].reshape(KT, P)]).transpose(2, 0, 1),
        "z_gain": a["gmlp_z_norm_g"].reshape(1, HALF),
        "out_gain": a["gmlp_out_g"].reshape(1, HALF),
        "subln_gain": a["subln_g"].reshape(1, VD),
        "final_gain": a["final_norm_g"].reshape(1, D),
        "lambdas": np.concatenate([a["lambda_q1"], a["lambda_k1"], a["lambda_q2"], a["lambda_k2"]], axis=1),
        "rope": rope.reshape(2, TT, P, ROT).transpose(2, 0, 1, 3),
    }
    arrays = {k: np.ascontiguousarray(w) for k, w in arrays.items()}
    nc = bacc.Bacc("TRN2", target_bir_lowering=False, num_devices=1)
    args = [nc.dram_tensor(k, w.shape, mybir.dt.from_np(w.dtype), kind="ExternalInput").ap() for k, w in arrays.items()]
    out = nc.dram_tensor("out", [T, D], FP32, kind="ExternalOutput").ap()
    hybrid_peer_block(nc, *args, out)
    got = run_bass_kernel_spmd(nc, [arrays], core_ids=[0]).results[0]["out"]
    return got.reshape(1, T, D)
```

```python
import math

import numpy as np
import concourse.bass as bass
from concourse import mybir
from contextlib import ExitStack

FP32 = mybir.dt.float32
FP32R = mybir.dt.float32r
U32 = mybir.dt.uint32
ALU = mybir.AluOpType
ACT = mybir.ActivationFunctionType
AX = mybir.AxisListType

P = 128
T, D = 256, 2048
TT = T // P
KT = D // P
HALF = D // 2
BANK = 512
HEADS, QK, VD = 8, 64, 128
ROT = 8
CHUNK = 64
GROUPS = 8
EPS = 1e-6
LAMBDA_INIT = 0.8 - 0.6 * math.exp(-0.3 * 0)
PH, TOPK, NKEYS = 8, 16, 128
HC = 2 * PH
FLOOR = -3.0e38
NEG = -1e30

UNIT = 1024
N_PROJ, N_OUT, N_WQ, N_U, N_V = 5 * KT, 2 * KT, 2 * HC, 2 * NKEYS, 2 * NKEYS
OUT0 = N_PROJ
WQ0 = OUT0 + N_OUT
U0 = WQ0 + N_WQ
V0 = U0 + N_U
RAW_SLOTS, HI_SLOTS, LO_SLOTS = 4, 4, 2
VG = 8
N_VG = NKEYS // VG
SPREAD_BANK = [(4 if s < VG // 2 else 0) + s % 2 for s in range(VG)]
Q_, K_, V_, Z_, U_ = range(5)
COLS = {Z_: 4096, U_: 3072, Q_: 0, K_: 1024, V_: 2048}
ATT0 = 3 * KT
COMBOS = TT * HEADS
STARTS = [3 * c // 2 for c in range(COMBOS)]
BESIDE0, BESIDE1 = ATT0, OUT0 + KT // 2
TOKB = 4
N_BATCH = T // TOKB
E2A = NKEYS // 2
PIECES = HC + 2 + PH + 2 * 7 + 1
PICKS_AT = (14, 24)
ROOTS_AT = (24, 27)
BESIDE_CHOICE = 2
GATES_AT = (10, 20)
BANK0 = (0, 4, 0, 4, 4)
PAIRS = NKEYS // 2
SPREAD1 = PAIRS - N_BATCH // 2
SPREAD2 = N_BATCH // VG


def hybrid_peer_block(nc, x, w_in, w_out, wq_t, keys_t, u_t, peer_v, ws_t, bs_t, gain_t, z_gain, out_gain,
                      subln_gain, final_gain, lambdas, rope, out):
    ctx = ExitStack()
    with ctx:
        base = (nc.sbuf_base + 63) // 64 * 64

        def at(name, off, shape, dt=FP32):
            return nc.alloc_sbuf_tensor_at(name, shape, dt, offset=base + off)

        def sem(name):
            return ctx.enter_context(nc.semaphore(name))

        KB = 1024
        store = at("store", 0, [P, NKEYS, T])
        X = at("X", 0, [P, TT, D])
        GRP = at("GRP", 16 * KB, [P, 5, TT, HALF])
        MIX = at("MIX", 56 * KB, [P, TT, D])
        QT = at("QT", 72 * KB, [P, HEADS, T])
        KTr = at("KTr", 80 * KB, [P, HEADS, T])
        PR = at("PR", 88 * KB, [P, 2, 2, T])
        AM = at("AM", 92 * KB, [P, 2, T])
        AT = at("AT", 94 * KB, [P, 2, P])
        XS = at("XS", 72 * KB, [P, TT, D])
        SQ = at("SQ", 96 * KB, [P, HALF])
        JUNK = at("JUNK", 100 * KB, [P, HALF])
        RT = at("RT", 104 * KB, [P, 4, 2 * HEADS, ROT])
        SQX = at("SQX", 88 * KB, [P, TT, D])
        ZG = at("ZG", 110 * KB, [P, HALF])
        OG = at("OG", 114 * KB, [P, HALF])
        WST = at("WST", 118 * KB, [P, GROUPS, P])
        SG = at("SG", 122 * KB, [P, VD])
        LAMV = at("LAMV", 123 * KB, [P, 4, QK])
        ROPE = at("ROPE", 124 * KB, [P, 2, TT, ROT])
        SC = at("SC", 64 * KB, [P, TT, HC, NKEYS])
        QTQ = at("QTQ", 80 * KB, [P, HC, T])
        KEYS = at("KEYS", 96 * KB, [P, HC, NKEYS])
        CAND = at("CAND", 104 * KB, [P, PH, TOPK, TOPK])
        EQ = at("EQ", 112 * KB, [P, PH, TOPK, TOPK])
        S16 = at("S16", 120 * KB, [P, TT, HC, TOPK])
        I16 = at("I16", 122 * KB, [P, TT, HC, TOPK], U32)
        I16F = at("I16F", 124 * KB, [P, TT, HC, TOPK])
        BEST = at("BEST", 126 * KB, [P, PH, TOPK])
        CI = at("CI", 126 * KB + 512, [P, PH, TOPK], U32)
        CIA = at("CIA", 127 * KB, [P, PH, TOPK], U32)
        CF = at("CF", 127 * KB + 512, [P, PH, TOPK])
        ROWS = at("ROWS", 62 * KB, [P, 3, PH * TOPK])
        xT = at("xT", 128 * KB, [P, KT, 2, T], FP32R)
        ACC = at("ACC", 128 * KB, [P, TT, D])
        WHL = at("WHL", 144 * KB, [P, VG, 2, T], FP32R)
        FG = at("FG", 0, [P, D])
        FJ = at("FJ", 8 * KB, [P, HALF])
        RAW = at("RAW", 160 * KB, [P, RAW_SLOTS, UNIT])
        HI = at("HI", 176 * KB, [P, HI_SLOTS, UNIT], FP32R)
        LO = at("LO", 192 * KB, [P, LO_SLOTS, UNIT], FP32R)
        off = [200 * KB]

        def small(name, shape, dt=FP32):
            n = 4 * int(np.prod(shape[1:]))
            t = at(name, off[0], shape, dt)
            off[0] += (n + 31) // 32 * 32
            return t

        IDENT = small("IDENT", [P, P])
        IOTA = small("IOTA", [P, NKEYS])
        EG = small("EG", [P, 3, T])
        GT = small("GT", [P, 2, KT])
        BS = small("BS", [P, GROUPS])
        SS = small("SS", [P, 10])
        GS = small("GS", [P, 2, 3, TT, GROUPS])
        LAM = small("LAM", [P, 8])
        NB = small("NB", [P, 2, 2])
        LS = small("LS", [P, 2, 2])
        RL = small("RL", [P, 2, 2])
        GM = small("GM", [P, 3, PH])
        ONE1 = small("ONE1", [P, TOKB, NKEYS])
        ONE2 = small("ONE2", [P, TOKB, E2A])

        PS = ctx.enter_context(nc.psum_tensor("PS", [P, 8, BANK], FP32))
        x1_dram = nc.dram_tensor("x1_spill", [T, D], FP32).ap()

        raw_ready = [sem(f"raw_ready{i}") for i in range(RAW_SLOTS)]
        hi_ready, used = sem("hi_ready"), sem("used")
        lo_ready = [sem(f"lo_ready{i}") for i in range(LO_SLOTS)]
        x_ready, small_ready = [sem(f"x_ready{i}") for i in range(2)], sem("small_ready")
        gain_ready, row_scales = sem("gain_ready"), sem("row_scales")
        consts = sem("consts")
        dve_chain = sem("dve_chain")
        sums0 = sem("sums0")
        warm = sem("warm")
        bank_done = sem("bank_done")
        sums = sem("sums")
        means = sem("means")
        roots = sem("roots")
        rows_ready = sem("rows_ready")
        tr_done, tr_hi, tr_lo = sem("tr_done"), sem("tr_hi"), sem("tr_lo")
        evac = sem("evac")
        z_ready, sz_done, sz_read = sem("z_ready"), sem("sz_done"), sem("sz_read")
        z_gelu = sem("z_gelu")
        roped, qk_tr, qk_out = sem("roped"), sem("qk_tr"), sem("qk_out")
        scored, maxed, exped = sem("scored"), sem("maxed"), sem("exped")
        lam_sums, lam_exp, mixed_probs = sem("lam_sums"), sem("lam_exp"), sem("mixed_probs")
        heads_ready = sem("heads_ready")
        at_done, at_out, pv_done, pv_out = sem("at_done"), sem("at_out"), sem("pv_done"), sem("pv_out")
        x1_ready, x1_saved, x1_back = sem("x1_ready"), sem("x1_saved"), sem("x1_back")
        tile_out = sem("tile_out")
        keys_ready = sem("keys_ready")
        sc_done, sc_out = sem("sc_done"), sem("sc_out")
        best_ready, gexp = sem("best_ready"), sem("gexp")
        picks, picks_tr, picks_out = sem("picks"), sem("picks_tr"), sem("picks_out")
        gelus = sem("gelus")
        one1, one2, one2g, g_done, g_read = sem("one1"), sem("one2"), sem("one2g"), sem("g_done"), sem("g_read")
        w_hi, w_lo, flushed = sem("w_hi"), sem("w_lo"), sem("flushed")
        scaled, act_scaled, gained = sem("scaled"), sem("act_scaled"), sem("gained")
        fg_ready, fin, stored = sem("fg_ready"), sem("fin"), sem("stored")

        v_view = peer_v.rearrange("(e j) d -> e j d", j=NKEYS)

        block = ctx.enter_context(nc.Block())

        @block.sync
        def _(sp):
            def former(slot, count):
                sp.wait_ge(lo_ready[slot % 2], count)

            def load(slot, src):
                sp.dma_start(RAW[:, slot, :], src).then_inc(raw_ready[slot], 16)

            sp.dma_start(X[:, 1, 0:HALF], x[P:T, 0:HALF]).then_inc(x_ready[0], 16)
            for n in range(KT):
                if n == 2:
                    for tt in range(TT):
                        sp.dma_start(X[:, tt, HALF:D], x[tt * P:(tt + 1) * P, HALF:D]).then_inc(x_ready[1], 16)
                if n >= RAW_SLOTS:
                    former(n % RAW_SLOTS, n // 2 - 1)
                load(n % RAW_SLOTS, w_in[n * P:(n + 1) * P, COLS[0]:COLS[0] + UNIT])

            def load_rows(w, first_unit, col):
                with sp.Fori(0, KT // 4) as i:
                    for r in range(4):
                        former(r, i * 2 + ((first_unit + r) // 2 - 1))
                        load(r, w[bass.ds(i * (4 * P) + r * P, P), col:col + UNIT])

            for g in range(1, 5):
                load_rows(w_in, g * KT, COLS[g])
            for g in range(2):
                load_rows(w_out, OUT0 + g * KT, g * UNIT)
            with sp.Fori(0, N_WQ // 4) as i:
                for r in range(4):
                    former(r, i * 2 + ((WQ0 + r) // 2 - 1))
                    load(r, wq_t[bass.ds(i * 2 + r // 2, 1), :, (r % 2) * UNIT:(r % 2 + 1) * UNIT]
                         .rearrange("a p n -> p (a n)"))
            with sp.Fori(0, N_U // 4) as i:
                for r in range(4):
                    former(r, i * 2 + ((U0 + r) // 2 - 1))
                    load(r, u_t[bass.ds(i * 2 + r // 2, 1), :, (r % 2) * UNIT:(r % 2 + 1) * UNIT]
                         .rearrange("a p n -> p (a n)"))
            with sp.Fori(0, N_VG) as g:
                for u in range(2 * VG):
                    h, jj = divmod(u, VG)
                    former(u, g * VG + ((V0 + u) // 2 - 1))
                    load(u % RAW_SLOTS,
                         v_view[:, bass.ds(g * VG + jj, 1), h * UNIT:(h + 1) * UNIT]
                         .rearrange("p a n -> p (a n)"))
            for tt in range(TT):
                for half, done in enumerate((act_scaled, fin)):
                    cols = slice(half * HALF, (half + 1) * HALF)
                    sp.wait_ge(done, tt + 1)
                    sp.dma_start(out[tt * P:(tt + 1) * P, cols], ACC[:, tt, cols]).then_inc(stored, 16)
            sp.wait_ge(stored, 16 * 2 * TT)

        @block.gpsimd
        def _(pool):
            nc.gpsimd.memset(IDENT[:], 0.0).then_inc(consts, 1)
            nc.gpsimd.iota(IOTA[:], [[1, NKEYS]], base=0, channel_multiplier=0,
                           allow_small_or_imprecise_dtypes=True).then_inc(consts, 1)
            pool.wait_ge(consts, 2)
            nc.gpsimd.affine_select(out=IDENT[:], in_=IDENT[:], compare_op=ALU.not_equal, fill=1.0, base=0,
                                    pattern=[[-1, P]], channel_multiplier=1).then_inc(consts, 1)
            pool.dma_start(GT[:], gain_t).then_inc(gain_ready, 16)
            loads = [
                (BS[:], bs_t), (WST[:], ws_t),
                (ZG[:], z_gain.broadcast_to([P, HALF])), (OG[:], out_gain.broadcast_to([P, HALF])),
                (SG[:], subln_gain.broadcast_to([P, VD])),
                (LAMV[:].rearrange("p a b -> p (a b)"), lambdas.broadcast_to([P, 4 * QK])),
                (ROPE[:], rope),
            ]
            pool.wait_ge(used, 2)
            for dst, src in loads:
                pool.dma_start(dst, src).then_inc(small_ready, 16)
            pool.wait_ge(small_ready, 16 * len(loads))
            pool.wait_ge(consts, 3)
            nc.gpsimd.memset(WST[CHUNK:P, :, 0:CHUNK], 0.0).then_inc(consts, 1)
            pool.wait_ge(consts, 4)
            for n in range(BESIDE0 + 1, BESIDE1, 2):
                pool.wait_ge(hi_ready, n + 1)
                pool.wait_ge(used, n - (LO_SLOTS - 1))
                nc.gpsimd.tensor_tensor(LO[:, n % 2, :], RAW[:, n % 4, :], HI[:, n % 4, :].bitcast(FP32),
                                        ALU.subtract).then_inc(lo_ready[n % 2], 1)
            pool.wait_ge(tr_lo, 24)
            pool.dma_start(KEYS[:], keys_t).then_inc(keys_ready, 16)
            pool.wait_ge(x1_ready, 8)
            for tt in range(TT):
                pool.dma_start(x1_dram[tt * P:(tt + 1) * P, :], X[:, tt, :]).then_inc(x1_saved, 16)
            with pool.Fori(BESIDE_CHOICE, SPREAD1) as i:
                for r in (1, 3):
                    pool.wait_ge(hi_ready, i * 4 + (U0 + r + 1))
                    pool.wait_ge(used, i * 4 + (U0 + r - (LO_SLOTS - 1)))
                    nc.gpsimd.tensor_tensor(LO[:, r % 2, :], RAW[:, r, :], HI[:, r, :].bitcast(FP32),
                                            ALU.subtract).then_inc(lo_ready[r % 2], 1)

            for of_both in (0, N_BATCH):
                with pool.Fori(0, N_BATCH) as b:
                    pool.wait_ge(one2, b + (of_both + 1))
                    nc.gpsimd.tensor_tensor(ONE2[:], ONE2[:], EG[:, 2, bass.ds(b * TOKB, TOKB)].unsqueeze(2)
                                            .broadcast_to([P, TOKB, E2A]), ALU.mult).then_inc(one2g, 1)
            pool.wait_ge(used, V0 + 16 * 9)
            pool.dma_start(FG[:], final_gain.broadcast_to([P, D])).then_inc(fg_ready, 16)

        @block.scalar
        def _(act):
            def hi_part(slot):
                nc.scalar.activation(HI[:, slot, :], RAW[:, slot, :], ACT.Copy).then_inc(hi_ready, 1)

            def hi(n):
                act.wait_ge(raw_ready[n % 4], 16 * (n // RAW_SLOTS + 1))
                if n >= HI_SLOTS:
                    act.wait_ge(used, n - (HI_SLOTS - 1))
                hi_part(n % 4)

            def hi_at(it, per, u):
                act.wait_ge(raw_ready[u % 4], it * (4 * per) + 16 * (u // 4 + 1))
                act.wait_ge(used, it * per + (u - (HI_SLOTS - 1)))
                hi_part(u % 4)

            n_sums = [0]

            def squares(src, col, junk):
                if n_sums[0]:
                    act.wait_ge(sums, n_sums[0])
                n_sums[0] += 1
                nc.scalar.activation(junk, src, ACT.Square, accum_out=SS[:, col:col + 1]).then_inc(sums, 1)

            def root(count, dst):
                act.wait_ge(means, count)
                nc.scalar.activation(dst, dst, ACT.Sqrt).then_inc(roots, 1)

            def transposed_hi(kp, bank, count, gain):
                act.wait_ge(tr_done, count)
                for k in (2 * kp, 2 * kp + 1):
                    src = PS[:, bank, (k % 2) * T:(k % 2 + 1) * T]
                    if gain is None:
                        ins = nc.scalar.activation(xT[:, k, 0, :], src, ACT.Copy)
                    else:
                        ins = nc.scalar.activation(xT[:, k, 0, :], src, ACT.Copy, scale=GT[:, gain, k:k + 1])
                ins.then_inc(tr_hi, 1)

            act.dma_start(X[:, 0, 0:HALF], x[0:P, 0:HALF]).then_inc(x_ready[0], 16)
            act.wait_ge(consts, 3)
            nc.scalar.activation(SS[:, 4:5], IDENT[:, 0:1], ACT.Copy).then_inc(warm, 1)
            act.wait_ge(gain_ready, 16)
            for kp in range(4):
                transposed_hi(kp, 4 + kp, kp + 1, 0)
                hi(kp)
            hi(4)
            for kp in range(4, 8):
                transposed_hi(kp, kp, kp + 1, 0)
                hi(kp + 1)
            def copy_out(g):
                act.wait_ge(row_scales, 1)
                for tt in range(TT):
                    for c in range(2):
                        act.wait_ge(used, KT * (g + 1))
                        nc.scalar.activation(GRP[:, g, tt, c * BANK:(c + 1) * BANK], PS[:, BANK0[g] + 2 * tt + c, :],
                                             ACT.Gelu_apprx_tanh if g == U_ else ACT.Copy,
                                             scale=SS[:, 8 + tt:9 + tt]).then_inc(evac, 1)

            def heads_out(b):
                act.wait_ge(qk_tr, b + 1)
                nc.scalar.activation((QT, KTr)[b // 4][:, 2 * (b % 4):2 * (b % 4) + 2, :],
                                     PS[:, b, :].rearrange("p (a b) -> p a b", a=2), ACT.Copy).then_inc(qk_out, 1)

            def exps(c):
                keys = P * (c // HEADS + 1)
                act.wait_ge(maxed, c + 1)
                if c >= 2:
                    act.wait_ge(mixed_probs, c - 1)
                for m in range(2):
                    ins = nc.scalar.activation(PR[:, c % 2, m, 0:keys], PS[:, m, 0:keys], ACT.Exp,
                                               bias=NB[:, c % 2, m:m + 1], scale=QK ** -0.5,
                                               accum_out=LS[:, c % 2, m:m + 1])
                ins.then_inc(exped, 1)

            def probs_out(c):
                tt = c // HEADS
                act.wait_ge(at_done, c + 1)
                if c:
                    act.wait_ge(pv_done, c)
                nc.scalar.activation(AT[:, 0:tt + 1, :], PS[:, 2, 0:P * (tt + 1)].rearrange("p (a b) -> p a b", b=P),
                                     ACT.Copy).then_inc(at_out, 1)

            def head_out(c):
                tt, h = divmod(c, HEADS)
                act.wait_ge(pv_done, c + 1)
                nc.scalar.activation(MIX[:, tt, h * VD:(h + 1) * VD], PS[:, 3, 0:VD], ACT.Copy).then_inc(pv_out, 1)

            act.wait_ge(x_ready[0], 16 * TT)
            act.wait_ge(x_ready[1], 16 * TT)
            for n in range(9, ATT0 + 4):
                hi(n)
                if n in (11, 13):
                    tt = (n - 11) // 2
                    nc.scalar.activation(SQX[:, tt, :], X[:, tt, :], ACT.Square, accum_out=SS[:, tt:tt + 1])\
                        .then_inc(sums0, 1)
                if n == 16:
                    root(1, SS[:, 6:8])
                if n % KT == 3 and n > KT:
                    copy_out(n // KT - 1)
                if n == 2 * KT:
                    act.wait_ge(lam_sums, 1)
                    nc.scalar.activation(LAM[:, 2:4], LAM[:, 0:2], ACT.Exp).then_inc(lam_exp, 1)
                for g in (K_, V_):
                    if 0 <= n - 5 - (g * KT + 8) < 4:
                        heads_out(4 * (g - 1) + n - 5 - (g * KT + 8))
            for m in range(2 * KT):
                if m in STARTS:
                    exps(STARTS.index(m))
                if m - 2 in STARTS:
                    probs_out(STARTS.index(m - 2))
                if m - 3 in STARTS:
                    head_out(STARTS.index(m - 3))
                hi(ATT0 + m + 4)
                if m == KT - 2:
                    copy_out(Z_)
                if m == STARTS[-1] + 1:
                    for tt in range(TT):
                        act.wait_ge(evac, 16)
                        nc.scalar.activation(GRP[:, Z_, tt, :], GRP[:, Z_, tt, :], ACT.Gelu_apprx_tanh).then_inc(z_gelu, 1)
                if m == ROOTS_AT[0]:
                    root(2, GS[:, 1, 1, 0, :])
                if m == ROOTS_AT[1]:
                    root(3, GS[:, 1, 1, 1, :])
                if m == 2 * KT - 3:
                    for kp in range(4):
                        transposed_hi(kp, kp, 8 + kp + 1, None)
                if m == 2 * KT - 2:
                    root(4, GS[:, 0, 1])
            copy_out(U_)
            hi(OUT0 + 4)
            hi(OUT0 + 5)
            act.wait_ge(sz_read, 16)
            for tt in range(TT):
                squares(MIX[:, tt, HALF:D], tt, JUNK[:])
            root(5, SS[:, 6:8])
            for n in range(OUT0 + 6, OUT0 + 10):
                hi(n)
            for kp in range(4, 8):
                transposed_hi(kp, kp, 8 + kp + 1, None)
            for n in range(OUT0 + 10, WQ0 + 4):
                hi(n)
                if n in (OUT0 + KT + 8, OUT0 + KT + 10):
                    tt = (n - OUT0 - KT - 8) // 2
                    act.wait_ge(x1_ready, 2 * tt + 2)
                    squares(X[:, tt, 0:HALF], tt, JUNK[:])
            for tt in range(TT):
                act.wait_ge(x1_ready, 4 + 2 * tt + 2)
                squares(X[:, tt, HALF:D], 2 + tt, JUNK[:])
                root(6 + tt, SS[:, 6 + tt:7 + tt])
            for kp in range(KT // 2):
                transposed_hi(kp, kp, 16 + kp + 1, 1)
            with act.Fori(0, N_WQ // 4) as i:
                for r in range(4):
                    hi_at(i, 4, WQ0 + 4 + r)

            def gelu(pair, count):
                act.wait_ge(tile_out, count)
                part = store[:, bass.ds(pair * 2, 2), :]
                nc.scalar.activation(part, part, ACT.Gelu_apprx_tanh).then_inc(gelus, 1)

            def first_scores_out(tt):
                for b in range(4):
                    act.wait_ge(sc_done, 4 * tt + b + 1)
                    nc.scalar.activation(SC[:, tt, 4 * b:4 * b + 4, :],
                                         PS[:, 4 + b, :].rearrange("p (a b) -> p a b", b=NKEYS), ACT.Copy).then_inc(sc_out, 1)

            def picks_to_rows(tt):
                act.wait_ge(picks_tr, tt + 1)
                nc.scalar.activation(EG[:, :, tt * P:(tt + 1) * P],
                                     PS[:, 7 - tt, 0:3 * P].rearrange("p (a b) -> p a b", b=P), ACT.Copy).then_inc(picks_out, 1)

            def pair_hi(i):
                for r in range(4):
                    hi_at(i, 4, U0 + r)

            def pairs(i, beside=None):
                pair_hi(i)
                if beside:
                    beside()
                gelu(i - 1, i * 2 + HC)

            def keys_scores_out():
                for tt in range(TT):
                    first_scores_out(tt)

            def gates_exp(tt):
                act.wait_ge(best_ready, tt + 1)
                nc.scalar.activation(ROWS[:, 2, :], ROWS[:, 2, :], ACT.Exp).then_inc(gexp, 1)

            beside = {1: keys_scores_out}
            for tt in range(TT):
                beside[GATES_AT[tt]] = lambda tt=tt: gates_exp(tt)
                beside[PICKS_AT[tt]] = lambda tt=tt: picks_to_rows(tt)
            plain_from = 1
            for special in sorted(beside) + [PAIRS]:
                if special > plain_from:
                    with act.Fori(plain_from, special) as i:
                        pairs(i)
                if special < PAIRS:
                    pairs(special, beside[special])
                plain_from = special + 1

            def weight_hi(g, s):
                act.wait_ge(used, g * 16 + (V0 - 16 + 9 + s))
                nc.scalar.activation(WHL[:, s, 0, :], store[:, bass.ds(g * VG + s, 1), :].rearrange("p a t -> p (a t)"),
                                     ACT.Copy).then_inc(w_hi, 1)

            for u in range(3):
                hi(V0 + u)
            act.wait_ge(x1_saved, 16 * TT)
            act.wait_ge(used, V0)
            for s in range(4):
                act.wait_ge(g_read, N_BATCH)
                weight_hi(0, s)
            for tt in range(TT):
                act.dma_start(ACC[:, tt, :], x1_dram[tt * P:(tt + 1) * P, :]).then_inc(x1_back, 16)
            gelu(PAIRS - 1, HC + NKEYS)

            def values(g, first=False, late=False, next_late=False, last=False):
                for u in range(2 * VG):
                    if not (first and u < 3):
                        hi_at(g, 2 * VG, V0 + u)
                    if late and u == 2:
                        act.wait_ge(g_read, 2 * N_BATCH)
                        for s in range(4):
                            weight_hi(g, s)
                    if late and u == 3:
                        for s in range(4, 8):
                            weight_hi(g, s)
                    if not late and u < 4:
                        weight_hi(g, u + 4)
                    if u >= 12 and not next_late:
                        weight_hi(g + 1, u - 12)
                    if last and u >= 2 * VG - 2:
                        tt = u - (2 * VG - 2)
                        act.wait_ge(fg_ready, 16)
                        act.wait_ge(flushed, 8 * N_VG - 6 + 2 * tt)
                        squares(ACC[:, tt, 0:HALF], tt, FJ[:])

            values(0, first=True)
            with act.Fori(1, SPREAD2 - 1) as g:
                values(g)
            values(SPREAD2 - 1, next_late=True)
            values(SPREAD2, late=True)
            with act.Fori(SPREAD2 + 1, N_VG - 1) as g:
                values(g)
            values(N_VG - 1, next_late=True, last=True)
            nc.scalar.activation(GM[:, 2, 0:1], GM[:, 1, 0:1], ACT.Sqrt).then_inc(warm, 1)

            def final_squares(tt):
                act.wait_ge(flushed, 8 * N_VG - 2 + 2 * tt)
                squares(ACC[:, tt, HALF:D], 2 + tt, FJ[:])

            def final_scale(tt):
                act.wait_ge(scaled, tt + 1)
                act.wait_ge(gained, tt + 1)
                nc.scalar.activation(ACC[:, tt, 0:HALF], ACC[:, tt, 0:HALF], ACT.Copy, scale=SS[:, 8 + tt:9 + tt])\
                    .then_inc(act_scaled, 1)

            final_squares(0)
            root(8, SS[:, 6:7])
            final_squares(1)
            final_scale(0)
            root(9, SS[:, 7:8])
            final_scale(1)

        @block.vector
        def _(dve):
            chain = [0]
            v = nc.vector

            def link(ins):
                chain[0] += 1
                ins.then_inc(dve_chain, 1)
                dve.wait_ge(dve_chain, chain[0])

            def split(u):
                v.tensor_tensor(LO[:, u % 2, :], RAW[:, u % 4, :], HI[:, u % 4, :].bitcast(FP32),
                                ALU.subtract).then_inc(lo_ready[u % 2], 1)

            def lo(n):
                if BESIDE0 <= n < BESIDE1 and n % 2:
                    return
                dve.wait_ge(hi_ready, n + 1)
                if n >= LO_SLOTS:
                    dve.wait_ge(used, n - (LO_SLOTS - 1))
                split(n)

            def lo_at(it, per, u):
                dve.wait_ge(hi_ready, it * per + (u + 1))
                dve.wait_ge(used, it * per + (u - (LO_SLOTS - 1)))
                split(u)

            def mean(dst, src, n):
                v.tensor_scalar(dst, src, 1.0 / n, EPS, ALU.mult, ALU.add).then_inc(means, 1)

            def transposed_lo(kp, bank, count, gain):
                dve.wait_ge(tr_hi, count)
                for k in (2 * kp, 2 * kp + 1):
                    src = PS[:, bank, (k % 2) * T:(k % 2 + 1) * T]
                    hi_part = xT[:, k, 0, :].bitcast(FP32)
                    if gain is None:
                        ins = v.tensor_tensor(xT[:, k, 1, :], src, hi_part, ALU.subtract)
                    else:
                        ins = v.scalar_tensor_tensor(xT[:, k, 1, :], src, GT[:, gain, k:k + 1], hi_part,
                                                     ALU.mult, ALU.subtract)
                ins.then_inc(tr_lo, 1)

            for kp in range(4):
                transposed_lo(kp, 4 + kp, kp + 1, 0)
                if kp < 2:
                    lo(kp)
            lo(2)
            for kp in range(4, 8):
                transposed_lo(kp, kp, kp + 1, 0)
                lo(kp - 1)
            dve.wait_ge(small_ready, 16 * 7)

            def group_sums(rows, which, tt):
                link(v.tensor_tensor(SQ[:], rows, rows, ALU.mult))
                link(v.tensor_reduce(GS[:, which, 0, tt, :], SQ[:].rearrange("p (a b) -> p a b", b=P), AX.X, ALU.add))

            def group_scale(rows, which, tt, gain):
                link(v.reciprocal(GS[:, which, 2, tt, :], GS[:, which, 1, tt, :]))
                by = rows.rearrange("p (a b) -> p a b", b=P)
                link(v.tensor_tensor(by, by, GS[:, which, 2, tt, :].unsqueeze(2).broadcast_to([P, 8, P]), ALU.mult))
                return v.tensor_tensor(by, by, gain, ALU.mult)

            def rotate(g, tt):
                rows = GRP[:, g, tt, :].rearrange("p (b d) -> p b d", d=QK)
                first, second = rows[:, :, 0:ROT], rows[:, :, ROT:2 * ROT]
                cos, sin = (ROPE[:, i, tt, :].unsqueeze(1).broadcast_to([P, 2 * HEADS, ROT]) for i in range(2))
                v.tensor_tensor(RT[:, 0], first, cos, ALU.mult)
                v.tensor_tensor(RT[:, 1], second, sin, ALU.mult)
                v.tensor_tensor(RT[:, 2], second, cos, ALU.mult)
                link(v.tensor_tensor(RT[:, 3], first, sin, ALU.mult))
                v.tensor_tensor(first, RT[:, 0], RT[:, 1], ALU.subtract)
                v.tensor_tensor(second, RT[:, 2], RT[:, 3], ALU.add).then_inc(roped, 1)
                dve.wait_ge(roped, 2 * g + tt + 1)

            def minus_lambda():
                maps = SQ[:, 0:2 * QK].rearrange("p (a b) -> p a b", a=2)
                link(v.tensor_tensor(maps, LAMV[:, 0:4:2, :], LAMV[:, 1:4:2, :], ALU.mult))
                v.tensor_reduce(LAM[:, 0:2], maps, AX.X, ALU.add).then_inc(lam_sums, 1)

            for n in range(7, ATT0 + 2):
                lo(n)
                if n == 12:
                    dve.wait_ge(sums0, TT)
                    mean(SS[:, 6:8], SS[:, 0:2], D)
                if n == 15:
                    dve.wait_ge(roots, 1)
                    v.reciprocal(SS[:, 8:10], SS[:, 6:8]).then_inc(row_scales, 1)
                for g in (Q_, K_):
                    if n in (KT * (g + 1) + 4, KT * (g + 1) + 6):
                        dve.wait_ge(evac, 4 * (g + 1))
                        rotate(g, (n - KT * (g + 1) - 4) // 2)
                if n == 2 * KT - 6:
                    minus_lambda()
            dve.wait_ge(lam_exp, 1)
            link(v.tensor_tensor(LAM[:, 4:5], LAM[:, 3:4], LAM[:, 2:3], ALU.subtract))
            link(v.tensor_scalar(LAM[:, 5:6], LAM[:, 4:5], -LAMBDA_INIT, None, ALU.add))

            def masked_max(c):
                tt = c // HEADS
                keys = P * (tt + 1)
                dve.wait_ge(scored, c + 1)
                link(v.memset(PS[0:CHUNK, 0:2, keys - CHUNK:keys], NEG))
                link(v.tensor_reduce(RL[:, c % 2, :], PS[:, 0:2, 0:keys], AX.X, ALU.max))
                v.tensor_scalar(NB[:, c % 2, :], RL[:, c % 2, :], -(QK ** -0.5), None, ALU.mult).then_inc(maxed, 1)

            def subtract_maps(c):
                keys = P * (c // HEADS + 1)
                dve.wait_ge(exped, c + 1)
                if c >= 2:
                    dve.wait_ge(at_done, c - 1)
                link(v.reciprocal(RL[:, c % 2, :], LS[:, c % 2, :]))
                link(v.tensor_tensor(RL[:, c % 2, 1:2], RL[:, c % 2, 1:2], LAM[:, 5:6], ALU.mult))
                link(v.tensor_scalar(PR[:, c % 2, 1, 0:keys], PR[:, c % 2, 1, 0:keys], RL[:, c % 2, 1:2], None, ALU.mult))
                v.scalar_tensor_tensor(AM[:, c % 2, 0:keys], PR[:, c % 2, 0, 0:keys], RL[:, c % 2, 0:1],
                                       PR[:, c % 2, 1, 0:keys], ALU.mult, ALU.add).then_inc(mixed_probs, 1)

            z_gain3 = ZG[:].rearrange("p (a b) -> p a b", b=P)
            s_gain3 = SG[:].unsqueeze(1).broadcast_to([P, HEADS, VD])
            heads_of = [MIX[:, tt, 0:HALF] for tt in range(TT)]
            z_of = [GRP[:, Z_, tt, :] for tt in range(TT)]
            link(v.tensor_scalar(SG[:], SG[:], 1.0 - LAMBDA_INIT, None, ALU.mult))

            def at_slot(m):
                if m == 15:
                    dve.wait_ge(pv_out, HEADS)
                    group_sums(heads_of[0], 1, 0)
                    mean(GS[:, 1, 1, 0, :], GS[:, 1, 0, 0, :], P)
                if m == 24:
                    dve.wait_ge(z_gelu, TT)
                    group_sums(z_of[0], 0, 0)
                if m == 25:
                    dve.wait_ge(roots, 2)
                    group_scale(heads_of[0], 1, 0, s_gain3)
                if m == 26:
                    dve.wait_ge(pv_out, COMBOS)
                    group_sums(heads_of[1], 1, 1)
                    mean(GS[:, 1, 1, 1, :], GS[:, 1, 0, 1, :], P)
                if m == 28:
                    dve.wait_ge(roots, 3)
                    group_scale(heads_of[1], 1, 1, s_gain3).then_inc(heads_ready, 1)

            for m in range(2 * KT - 1):
                lo(ATT0 + m + 2)
                if m - 1 in STARTS:
                    subtract_maps(STARTS.index(m - 1))
                if m in STARTS:
                    masked_max(STARTS.index(m))
                at_slot(m)
                if m == 2 * KT - 3:
                    for kp in range(4):
                        transposed_lo(kp, kp, 8 + kp + 1, None)
                    group_sums(z_of[1], 0, 1)
                    mean(GS[:, 0, 1], GS[:, 0, 0], P)
            dve.wait_ge(roots, 4)
            group_scale(z_of[0], 0, 0, z_gain3).then_inc(z_ready, 1)
            lo(OUT0 + 2)
            group_scale(z_of[1], 0, 1, z_gain3).then_inc(z_ready, 1)
            for tt in range(TT):
                for g in range(GROUPS):
                    dve.wait_ge(sz_done, 2 * tt + g // 4 + 1)
                    v.scalar_tensor_tensor(MIX[:, tt, HALF + g * P:HALF + (g + 1) * P],
                                           PS[:, 4 + 2 * tt + g // 4, (g % 4) * P:(g % 4 + 1) * P],
                                           BS[:, g:g + 1], GRP[:, U_, tt, g * P:(g + 1) * P],
                                           ALU.add, ALU.mult).then_inc(sz_read, 1)
                lo(OUT0 + 4 + tt)
            dve.wait_ge(sums, 2)
            mean(SS[:, 6:8], SS[:, 0:2], HALF)
            dve.wait_ge(roots, 5)
            link(v.reciprocal(SS[:, 8:10], SS[:, 6:8]))
            lo(OUT0 + 6)
            for tt in range(TT):
                v.scalar_tensor_tensor(MIX[:, tt, HALF:D], MIX[:, tt, HALF:D], SS[:, 8 + tt:9 + tt], OG[:],
                                       ALU.mult, ALU.mult).then_inc(rows_ready, 1)
            for kp in range(4, 8):
                transposed_lo(kp, kp, 8 + kp + 1, None)
            def residual(g, b):
                tt, c = divmod(b, 2)
                cols = slice(g * UNIT + c * BANK, g * UNIT + (c + 1) * BANK)
                if g == 1:
                    dve.wait_ge(*((bank_done, b + 1) if b < 3 else (used, WQ0)))
                v.tensor_tensor(X[:, tt, cols], PS[:, 4 * g + b, :], X[:, tt, cols], ALU.add).then_inc(x1_ready, 1)

            for n in range(OUT0 + 8, WQ0 + 1):
                lo(n)
                if OUT0 + KT + 2 <= n < OUT0 + KT + 6:
                    residual(0, n - OUT0 - KT - 2)
            for b in range(4):
                residual(1, b)
            for tt in range(TT):
                dve.wait_ge(sums, 4 + tt + 1)
                link(v.tensor_tensor(SS[:, 4 + tt:5 + tt], SS[:, tt:tt + 1], SS[:, 2 + tt:3 + tt], ALU.add))
                mean(SS[:, 6 + tt:7 + tt], SS[:, 4 + tt:5 + tt], D)
                dve.wait_ge(roots, 6 + tt)
                link(v.reciprocal(SS[:, 8 + tt:9 + tt], SS[:, 6 + tt:7 + tt]))
                for half in range(2):
                    cols = slice(half * HALF, (half + 1) * HALF)
                    v.tensor_scalar(XS[:, tt, cols], X[:, tt, cols], SS[:, 8 + tt:9 + tt], None, ALU.mult)\
                        .then_inc(rows_ready, 1)
            lo(WQ0 + 1)
            for kp in range(KT // 2):
                transposed_lo(kp, kp, 16 + kp + 1, 1)

            def add_halves(dst, bank):
                v.tensor_reduce(dst, PS[:, bank, :].rearrange("p (a t) -> p t a", a=2), AX.X, ALU.add).then_inc(tile_out, 1)

            with dve.Fori(0, N_WQ // 4) as i:
                for r in range(4):
                    lo_at(i, 4, WQ0 + 2 + r)
                    if r % 2:
                        dve.wait_ge(used, i * 4 + (WQ0 + r + 1))
                        add_halves(QTQ[:, bass.ds(i * 2 + r // 2, 1), :].rearrange("p a t -> p (a t)"), r // 2)

            grid = [P, PH // 2, TOPK, TOPK]

            def top16(row, values, places):
                link(v.max(values[:, 0:8], row))
                v.max_index(places[:, 0:8], values[:, 0:8], row)
                link(v.match_replace(row, values[:, 0:8], row, FLOOR))
                link(v.max(values[:, 8:16], row))
                link(v.max_index(places[:, 8:16], values[:, 8:16], row))

            def choice(tt):
                for c in range(HC):
                    dve.wait_ge(sc_out, 4 * tt + c // 4 + 1)
                    top16(SC[:, tt, c, :], S16[:, tt, c, :], I16[:, tt, c, :])
                    yield
                link(v.tensor_copy(I16F[:, tt], I16[:, tt]))
                s1, s2 = S16[:, tt, 0:HC:2, :], S16[:, tt, 1:HC:2, :]
                lists = I16F[:, tt, 0:HC:2, :], I16F[:, tt, 1:HC:2, :]
                heads = [slice(0, PH // 2), slice(PH // 2, PH)]
                for hs in heads:
                    link(v.tensor_tensor(CAND[:, hs], s1[:, hs].unsqueeze(3).broadcast_to(grid),
                                         s2[:, hs].unsqueeze(2).broadcast_to(grid), ALU.add))
                    yield
                for h in range(PH):
                    top16(CAND[:, h].rearrange("p a b -> p (a b)"), BEST[:, h], CI[:, h])
                    yield
                if tt:
                    dve.wait_ge(picks_tr, 1)
                gates = ROWS[:, 2].rearrange("p (h k) -> p h k", h=PH)
                v.tensor_tensor(gates, BEST[:], BEST[:, :, 0:1].broadcast_to([P, PH, TOPK]), ALU.subtract)\
                    .then_inc(best_ready, 1)
                for half, (op, by) in enumerate(((ALU.logical_shift_right, 4), (ALU.bitwise_and, 15))):
                    link(v.tensor_scalar(CIA[:], CI[:], by, None, op))
                    link(v.tensor_copy(CF[:], CIA[:]))
                    yield
                    for hs in heads:
                        link(v.tensor_tensor(EQ[:, hs], CF[:, hs].unsqueeze(3).broadcast_to(grid),
                                             IOTA[:, 0:TOPK].unsqueeze(1).unsqueeze(1).broadcast_to(grid), ALU.is_equal))
                        yield
                        link(v.tensor_tensor(EQ[:, hs], EQ[:, hs], lists[half][:, hs].unsqueeze(2).broadcast_to(grid), ALU.mult))
                        yield
                        link(v.tensor_reduce(ROWS[:, half].rearrange("p (h k) -> p h k", h=PH)[:, hs], EQ[:, hs], AX.X, ALU.add))
                        yield
                dve.wait_ge(gexp, tt + 1)
                link(v.tensor_reduce(GM[:, 0, :], gates, AX.X, ALU.add))
                link(v.reciprocal(GM[:, 1, :], GM[:, 0, :]))
                v.tensor_tensor(gates, gates, GM[:, 1, :].unsqueeze(2).broadcast_to([P, PH, TOPK]), ALU.mult).then_inc(picks, 1)
                yield

            def score(j, bank, units):
                dve.wait_ge(used, units)
                add_halves(store[:, bass.ds(j, 1), :].rearrange("p a t -> p (a t)"), bank)

            for n in (U0 + 2, U0 + 3):
                lo(n)
            dve.wait_ge(x1_saved, 16 * TT)
            score(0, 0, U0 + 2)

            pieces = choice(0), choice(1)
            done = [0, 0]

            def piece(i):
                tt = 0 if done[0] < PIECES else 1
                if done[tt] < PIECES:
                    next(pieces[tt])
                    done[tt] += 1

            for i in range(1, SPREAD1):
                for r in range(4):
                    if r % 2 == 0 or i < BESIDE_CHOICE:
                        lo_at(i, 4, U0 + r)
                    if r == 1:
                        score(2 * i - 1, 1, 4 * i + U0)
                    if r == 3:
                        score(2 * i, 0, 4 * i + U0 + 2)
                    if i >= BESIDE_CHOICE:
                        piece(i)
            assert done == [PIECES, PIECES]
            dve.wait_ge(picks_out, TT)

            def one_hot(dst, row, b, count, j0, signal):
                width = dst.shape[-1]
                dve.wait_ge(g_done, count)
                v.tensor_tensor(dst[:], IOTA[:, j0:j0 + width].unsqueeze(1).broadcast_to([P, TOKB, width]),
                                EG[:, row, bass.ds(b * TOKB, TOKB)].unsqueeze(2).broadcast_to([P, TOKB, width]),
                                ALU.is_equal).then_inc(signal, 1)

            def apply_gates(b, bank, j0, count):
                dve.wait_ge(g_done, count + 1)
                part = store[:, j0:j0 + E2A, bass.ds(b * TOKB, TOKB)]
                v.tensor_tensor(part, part, PS[:, bank, 0:TOKB * E2A]
                                .rearrange("p (t j) -> p j t", t=TOKB), ALU.mult).then_inc(g_read, 1)

            def pair(i, first=False):
                for r in range(4):
                    lo_at(i, 4, U0 + r)
                    b = (i - SPREAD1) * 2 + r // 2
                    if r % 2 == 0:
                        one_hot(ONE2, 1, b, b, 0, one2)
                        one_hot(ONE1, 0, b, b, 0, one1)
                        if first and r == 2:
                            dve.wait_ge(gelus, SPREAD1)
                        if not (first and r == 0):
                            apply_gates(b - 1, 2 + (r // 2 + 1) % 2, 0, b - 1)
                    if r == 1:
                        score(i * 2 - 1, 1, i * 4 + U0)
                    if r == 3:
                        score(i * 2, 0, i * 4 + (U0 + 2))

            pair(SPREAD1, first=True)
            with dve.Fori(SPREAD1 + 1, PAIRS) as i:
                pair(i)

            def weight_lo(g, s):
                dve.wait_ge(w_hi, g * VG + (s + 1))
                v.tensor_tensor(WHL[:, s, 1, :], store[:, bass.ds(g * VG + s, 1), :].rearrange("p a t -> p (a t)"),
                                WHL[:, s, 0, :].bitcast(FP32), ALU.subtract).then_inc(w_lo, 1)

            def flush(g, h, b, onto_first, final=False):
                if final and b < 3:
                    dve.wait_ge(bank_done, 3 + b + 1)
                else:
                    dve.wait_ge(used, g * 16 + (V0 + 8 * h + 8))
                tt, c = divmod(b, 2)
                cols = slice(h * UNIT + c * BANK, h * UNIT + (c + 1) * BANK)
                if not onto_first:
                    dve.wait_ge(flushed, g * 8 + (4 * h + b - 7))
                v.tensor_tensor(ACC[:, tt, cols], PS[:, 4 * h + b, :], ACC[:, tt, cols], ALU.add).then_inc(flushed, 1)

            def values(g, first=False, second=False, spread=True, late=False, next_late=False):
                for u in range(2 * VG):
                    lo_at(g, 2 * VG, V0 + u)
                    if u % 2 == 0 and (spread or late and u == 0):
                        b = g * VG + u // 2
                        s = (u // 2 - 1) % VG
                        if spread:
                            one_hot(ONE2, 1, b, b + N_BATCH, E2A, one2)
                            one_hot(ONE1, 0, b, b + N_BATCH, 0, one1)
                        if first and u == 0:
                            apply_gates(N_BATCH - 1, 3, 0, N_BATCH - 1)
                        else:
                            if first and u == 2:
                                dve.wait_ge(gelus, PAIRS)
                            apply_gates(b - 1, SPREAD_BANK[s], E2A, b + (N_BATCH - 1))
                    if u == 0 and (first or late):
                        if first:
                            score(NKEYS - 1, 1, V0)
                        for s in range(4):
                            weight_lo(g, s)
                    if u < 4:
                        weight_lo(g, u + 4)
                    if u >= 12 and not next_late:
                        weight_lo(g + 1, u - 12)
                    if u % 2 and u < VG and not first:
                        flush(g - 1, 1, u // 2, second)
                    if u % 2 and u > VG:
                        if first and u == VG + 1:
                            dve.wait_ge(x1_back, 16 * TT)
                        flush(g, 0, u // 2 - 4, first)

            values(0, first=True)
            values(1, second=True)
            with dve.Fori(2, SPREAD2 - 1) as g:
                values(g)
            values(SPREAD2 - 1, next_late=True)
            values(SPREAD2, spread=False, late=True)
            with dve.Fori(SPREAD2 + 1, N_VG - 1) as g:
                values(g, spread=False)
            values(N_VG - 1, spread=False, next_late=True)
            dve.wait_ge(fg_ready, 16)
            for tt in range(TT):
                dve.wait_ge(sums, 6 + tt + 1)
                v.tensor_tensor(ACC[:, tt, 0:HALF], ACC[:, tt, 0:HALF], FG[:, 0:HALF], ALU.mult).then_inc(gained, 1)

            def final_mean(tt):
                dve.wait_ge(sums, 8 + tt + 1)
                link(v.tensor_tensor(SS[:, 4 + tt:5 + tt], SS[:, tt:tt + 1], SS[:, 2 + tt:3 + tt], ALU.add))
                mean(SS[:, 6 + tt:7 + tt], SS[:, 4 + tt:5 + tt], D)

            def final_scale(tt):
                dve.wait_ge(roots, 8 + tt)
                v.reciprocal(SS[:, 8 + tt:9 + tt], SS[:, 6 + tt:7 + tt]).then_inc(scaled, 1)
                dve.wait_ge(scaled, tt + 1)
                v.scalar_tensor_tensor(ACC[:, tt, HALF:D], ACC[:, tt, HALF:D], SS[:, 8 + tt:9 + tt], FG[:, HALF:D],
                                       ALU.mult, ALU.mult).then_inc(fin, 1)

            for b in range(4):
                flush(N_VG - 1, 1, b, False, final=True)
                if b == 2:
                    final_mean(0)
            final_scale(0)
            final_mean(1)
            final_scale(1)

        @block.tensor
        def _(pe):
            mm = nc.tensor.matmul

            def transpose_tiles(src, tiles, bank, tt):
                for k in tiles:
                    b = bank + (k - tiles[0]) // 2
                    last = nc.tensor.transpose(PS[:, b, (k % 2) * T + tt * P:(k % 2) * T + (tt + 1) * P],
                                               src[:, tt, k * P:(k + 1) * P], IDENT[:])
                    if tt == TT - 1 and k % 2:
                        last.then_inc(tr_done, 1)

            def row_unit(u, bank, high, low, first, last, low_ready, free=None, by_bank=False):
                h, l = HI[:, u % 4, :], LO[:, u % 2, :]
                halves = [slice(c * BANK, (c + 1) * BANK) for c in range(2)]
                for tt in range(TT):
                    banks = [PS[:, bank + 2 * tt + c, :] for c in range(2)]
                    if free:
                        free(tt)
                    if by_bank:
                        low_ready()
                        for c in range(2):
                            mm(banks[c], high(tt), h[:, halves[c]], start=first, stop=False)
                            mm(banks[c], high(tt), l[:, halves[c]], start=False, stop=False)
                            ins = mm(banks[c], low(tt), h[:, halves[c]], start=False, stop=last)
                            if 2 * tt + c < 3:
                                ins.then_inc(bank_done, 1)
                        continue
                    for c in range(2):
                        mm(banks[c], high(tt), h[:, halves[c]], start=first, stop=False)
                    if tt:
                        for c in range(2):
                            mm(banks[c], high(tt), l[:, halves[c]], start=False, stop=False)
                    for c in range(2):
                        ins = mm(banks[c], low(tt), h[:, halves[c]], start=False, stop=last and tt > 0)
                    if not tt:
                        low_ready()
                        for c in range(2):
                            mm(banks[c], high(tt), l[:, halves[c]], start=False, stop=last)
                ins.then_inc(used, 1)

            def column_unit(u, bank, low_ready, ready=None):
                def tile(kk):
                    return (KT // 2) * (u % 2) + kk, slice(kk * P, (kk + 1) * P)

                def high_part(kk):
                    k, cols = tile(kk)
                    if ready:
                        ready(k)
                    return mm(PS[:, bank, :], HI[:, u % 4, cols], xT[:, k].rearrange("p a t -> p (a t)"),
                              start=k == 0, stop=k == KT - 1)

                for kk in range(7):
                    high_part(kk)
                low_ready()
                for kk in range(8):
                    k, cols = tile(kk)
                    if ready:
                        ready(k)
                    mm(PS[:, bank, 0:T], LO[:, u % 2, cols], xT[:, k, 0, :], start=False, stop=False)
                high_part(7).then_inc(used, 1)

            def x_part(k, part):
                return lambda tt: xT[:, k, part, tt * P:(tt + 1) * P]

            def high_ready(n):
                pe.wait_ge(hi_ready, n + 1)

            def low_ready(n):
                return lambda: pe.wait_ge(lo_ready[n % 2], n // 2 + 1)

            pe.wait_ge(consts, 3)
            for tt in range(TT):
                pe.wait_ge(x_ready[0], 16 * TT)
                transpose_tiles(X, range(8), 4, tt)

            def heads_transposed(b):
                g = (Q_, K_)[b // 4]
                pe.wait_ge(roped, 2 * g + 2)
                for h in (2 * (b % 4), 2 * (b % 4) + 1):
                    for tt in range(TT):
                        last = nc.tensor.transpose(PS[:, b, (h % 2) * T + tt * P:(h % 2) * T + (tt + 1) * P],
                                                   GRP[:, g, tt, h * P:(h + 1) * P], IDENT[:])
                last.then_inc(qk_tr, 1)

            def scores(c):
                tt, h = divmod(c, HEADS)
                keys = P * (tt + 1)
                if c:
                    pe.wait_ge(exped, c)
                for m in range(2):
                    half = slice(QK * m, QK * (m + 1))
                    last = mm(PS[:, m, 0:keys], QT[half, h, tt * P:(tt + 1) * P], KTr[half, h, 0:keys],
                              start=True, stop=True)
                last.then_inc(scored, 1)

            def probs_transposed(c):
                pe.wait_ge(mixed_probs, c + 1)
                if c:
                    pe.wait_ge(at_out, c)
                for kt in range(c // HEADS + 1):
                    last = nc.tensor.transpose(PS[:, 2, kt * P:(kt + 1) * P], AM[:, c % 2, kt * P:(kt + 1) * P], IDENT[:])
                last.then_inc(at_done, 1)

            def times_values(c):
                tt, h = divmod(c, HEADS)
                pe.wait_ge(at_out, c + 1)
                if c:
                    pe.wait_ge(pv_out, c)
                for kt in range(tt + 1):
                    last = mm(PS[:, 3, 0:VD], AT[:, kt, :], GRP[:, V_, kt, h * VD:(h + 1) * VD],
                              start=kt == 0, stop=kt == tt)
                last.then_inc(pv_done, 1)

            for g in range(5):
                for k in range(KT):
                    n = g * KT + k
                    free = None
                    if g == 0:
                        pe.wait_ge(tr_lo, k // 2 + 1)
                    if g == 1 and k == 0:
                        pe.wait_ge(tr_lo, 8)
                    if k == 0 and g in (V_, U_):
                        pe.wait_ge(evac, 4 * (g - 1))
                        if g == U_:
                            def free(tt):
                                pe.wait_ge(evac, 4 * Z_ + 2 * tt + 2)
                    if k == 0 and g == V_:
                        pe.wait_ge(qk_out, 4)
                    if k == 0 and g == Z_:
                        pe.wait_ge(qk_out, 8)
                    high_ready(n)
                    row_unit(n, BANK0[g], x_part(k, 0), x_part(k, 1), k == 0, k == KT - 1, low_ready(n), free)
                    if g == Q_ and k == 1:
                        pe.wait_ge(tr_lo, 4)
                        pe.wait_ge(x_ready[1], 16 * TT)
                        for tt in range(TT):
                            transpose_tiles(X, range(8, KT), 4, tt)
                    if g in (K_, V_) and 8 <= k < 12:
                        heads_transposed(4 * (g - 1) + k - 8)
                    if g in (Z_, U_):
                        m = n - ATT0
                        if m in STARTS:
                            if m == 0:
                                pe.wait_ge(evac, 12)
                            scores(STARTS.index(m))
                        if m - 3 in STARTS:
                            times_values(STARTS.index(m - 3))
                        if m - 2 in STARTS:
                            probs_transposed(STARTS.index(m - 2))
                        if m == 2 * KT - 3:
                            pe.wait_ge(pv_out, COMBOS)
                            pe.wait_ge(heads_ready, 1)
                            for tt in range(TT):
                                transpose_tiles(MIX, range(8), 0, tt)

            def mix_positions():
                pe.wait_ge(consts, 4)
                pe.wait_ge(evac, 20)
                for tt in range(TT):
                    pe.wait_ge(z_ready, tt + 1)
                    for g in range(GROUPS):
                        last = mm(PS[:, 4 + 2 * tt + g // 4, (g % 4) * P:(g % 4 + 1) * P], WST[:, g, :],
                                  GRP[:, Z_, tt, g * P:(g + 1) * P], start=True, stop=True)
                        if g % 4 == 3:
                            last.then_inc(sz_done, 1)

            for g in range(2):
                for k in range(KT):
                    n = OUT0 + g * KT + k
                    if g == 0:
                        pe.wait_ge(tr_lo, 8 + max(4, k // 2 + 1))
                        if k == 2:
                            mix_positions()
                        if k == 7:
                            pe.wait_ge(sz_read, 16)
                            pe.wait_ge(rows_ready, 2)
                            for tt in range(TT):
                                transpose_tiles(MIX, range(8, 16), 4, tt)
                    elif k == 0:
                        pe.wait_ge(tr_lo, 16)
                    high_ready(n)
                    row_unit(n, 4 * g, x_part(k, 0), x_part(k, 1), k == 0, k == KT - 1, low_ready(n),
                             by_bank=n == WQ0 - 1)
            pe.wait_ge(x1_ready, 8)
            for tt, half in ((0, 0), (0, 1), (1, 0), (1, 1)):
                pe.wait_ge(rows_ready, 2 + 2 * tt + half + 1)
                transpose_tiles(XS, range(8 * half, 8 * half + 8), 4 * half, tt)
            def query_pair(i, first=False):
                for r in range(4):
                    pe.wait_ge(hi_ready, i * 4 + (WQ0 + r + 1))
                    if r % 2 == 0 and not first:
                        pe.wait_ge(tile_out, i * 2 + (r // 2 - 1))
                    column_unit(r, r // 2, lambda: pe.wait_ge(lo_ready[r % 2], i * 2 + ((WQ0 + r) // 2 + 1)),
                                (lambda k: pe.wait_ge(tr_lo, 16 + max(2, k // 2 + 1))) if first and r < 2 else None)

            query_pair(0, first=True)
            with pe.Fori(1, N_WQ // 4) as i:
                query_pair(i)

            def spread(bank, count, again=True):
                pe.wait_ge(one1, count + 1)
                pe.wait_ge(one2g, count + 1)
                if again:
                    pe.wait_ge(g_read, count - 1)
                for t in range(TOKB):
                    last = mm(PS[:, bank, t * E2A:(t + 1) * E2A], ONE1[:, t, :], ONE2[:, t, :],
                              start=True, stop=True)
                last.then_inc(g_done, 1)

            def pair(i, spreads=False, first=False):
                for r in range(4):
                    pe.wait_ge(hi_ready, i * 4 + (U0 + r + 1))
                    if r % 2 == 0:
                        pe.wait_ge(tile_out, i * 2 + (HC + r // 2 - 1))
                    column_unit(r, r // 2, lambda: pe.wait_ge(lo_ready[r % 2], i * 2 + ((U0 + r) // 2 + 1)))
                    if spreads and r % 2 == 0:
                        spread(2 + r // 2, (i - SPREAD1) * 2 + r // 2, again=not first)

            def picks_transposed(tt):
                pe.wait_ge(picks, tt + 1)
                for r in range(3):
                    last = nc.tensor.transpose(PS[:, 7 - tt, r * P:(r + 1) * P], ROWS[:, r, :], IDENT[:])
                last.then_inc(picks_tr, 1)

            pair(0)
            pe.wait_ge(tile_out, HC)
            pe.wait_ge(keys_ready, 16)
            for tt in range(TT):
                for b in range(4):
                    if tt:
                        pe.wait_ge(sc_out, b + 1)
                    for c in range(4 * b, 4 * b + 4):
                        last = mm(PS[:, 4 + b, (c % 4) * NKEYS:(c % 4 + 1) * NKEYS], QTQ[:, c, tt * P:(tt + 1) * P],
                                  KEYS[:, c, :], start=True, stop=True)
                    last.then_inc(sc_done, 1)
            with pe.Fori(1, PICKS_AT[0]) as i:
                pair(i)
            pe.wait_ge(sc_out, 8)
            picks_transposed(0)
            with pe.Fori(PICKS_AT[0], PICKS_AT[1]) as i:
                pair(i)
            picks_transposed(1)
            with pe.Fori(PICKS_AT[1], SPREAD1) as i:
                pair(i)

            pair(SPREAD1, spreads=True, first=True)
            with pe.Fori(SPREAD1 + 1, PAIRS) as i:
                pair(i, spreads=True)
            pe.wait_ge(tile_out, HC + NKEYS - 1)

            def values(g, first=False, spreads=True, last=False):
                for u in range(2 * VG):
                    h, jj = divmod(u, VG)
                    pe.wait_ge(hi_ready, g * 2 * VG + (V0 + u + 1))
                    if h == 0:
                        pe.wait_ge(w_lo, g * VG + (jj + 1))
                    if jj == 0 and not first:
                        pe.wait_ge(flushed, g * 8 + (4 * h - 4))
                    if jj == 0 and first and h == 0:
                        pe.wait_ge(tile_out, HC + NKEYS)
                    if jj == 0 and spreads:
                        pe.wait_ge(g_read, g * VG + (N_BATCH + 4 * h))
                    row_unit(u, 4 * h, lambda tt: WHL[:, jj, 0, tt * P:(tt + 1) * P],
                             lambda tt: WHL[:, jj, 1, tt * P:(tt + 1) * P], jj == 0, jj == VG - 1,
                             lambda: pe.wait_ge(lo_ready[u % 2], g * VG + ((V0 + u) // 2 + 1)),
                             by_bank=last and u == 2 * VG - 1)
                    if spreads and u % 2 == 0:
                        s = u // 2
                        if s % 4 < 2 and not (first and s < 2):
                            pe.wait_ge(flushed, g * 8 + s - 3)
                        spread(SPREAD_BANK[s], g * VG + (N_BATCH + s))

            values(0, first=True)
            with pe.Fori(1, SPREAD2) as g:
                values(g)
            pe.wait_ge(g_read, 2 * N_BATCH)
            with pe.Fori(SPREAD2, N_VG - 1) as g:
                values(g, spreads=False)
            values(N_VG - 1, spreads=False, last=True)


def kernel(**inputs):
    import concourse.bacc as bacc
    from concourse.bass_utils import run_bass_kernel_spmd

    a = {k: np.asarray(w) for k, w in inputs.items()}
    inv = (500000.0 ** (-np.arange(0, 2 * ROT, 2, dtype=np.float32) / np.float32(2 * ROT))).astype(np.float32)
    ang = np.arange(T, dtype=np.float32)[:, None] * inv[None, :]
    rope = np.stack([np.cos(ang), np.sin(ang)]).astype(np.float32)
    arrays = {
        "x": a["x"].reshape(T, D),
        "w_in": a["w_in"][0],
        "w_out": a["w_out"][0],
        "wq_t": a["peer_w_q"][0].reshape(KT, P, HC, P).transpose(2, 1, 0, 3).reshape(HC, P, D),
        "keys_t": a["peer_sub_keys"][0].transpose(3, 0, 1, 2).reshape(P, HC, NKEYS),
        "u_t": a["peer_u"][0].reshape(NKEYS, NKEYS, KT, P).transpose(1, 3, 2, 0).reshape(NKEYS, P, D),
        "peer_v": a["peer_v"][0],
        "ws_t": a["gmlp_w_s"][0].transpose(2, 0, 1),
        "bs_t": a["gmlp_b_s"][0].T,
        "gain_t": np.stack([a["mix_norm_g"][0].reshape(KT, P), a["ffn_norm_g"][0].reshape(KT, P)]).transpose(2, 0, 1),
        "z_gain": a["gmlp_z_norm_g"].reshape(1, HALF),
        "out_gain": a["gmlp_out_g"].reshape(1, HALF),
        "subln_gain": a["subln_g"].reshape(1, VD),
        "final_gain": a["final_norm_g"].reshape(1, D),
        "lambdas": np.concatenate([a["lambda_q1"], a["lambda_k1"], a["lambda_q2"], a["lambda_k2"]], axis=1),
        "rope": rope.reshape(2, TT, P, ROT).transpose(2, 0, 1, 3),
    }
    arrays = {k: np.ascontiguousarray(w) for k, w in arrays.items()}
    nc = bacc.Bacc("TRN2", target_bir_lowering=False, num_devices=1)
    args = [nc.dram_tensor(k, w.shape, mybir.dt.from_np(w.dtype), kind="ExternalInput").ap() for k, w in arrays.items()]
    out = nc.dram_tensor("out", [T, D], FP32, kind="ExternalOutput").ap()
    hybrid_peer_block(nc, *args, out)
    got = run_bass_kernel_spmd(nc, [arrays], core_ids=[0]).results[0]["out"]
    return got.reshape(1, T, D)
```
